# Optimizing a Trainium2 kernel written in Bass

```python
import jax, jax.numpy as jnp
from jax import lax
import numpy as np

D_MODEL = 2048
BATCH = 1
SEQ = 512
DEPTH = 1

D_MIX = D_MODEL
ATTN_WIDTH = D_MIX // 2
LRU_WIDTH = D_MIX - ATTN_WIDTH
ATTN_HEAD_DIM = 128
ATTN_HEADS = ATTN_WIDTH // ATTN_HEAD_DIM
LRU_BLOCKS = 8
LRU_BLOCK_W = LRU_WIDTH // LRU_BLOCKS
CONV_W = 4
LRU_C = 8.0
Q_BLOCK = 128
NORM_EPS = 1e-6
N_IN = 3 * ATTN_WIDTH + ATTN_HEADS + ATTN_WIDTH + LRU_WIDTH + LRU_WIDTH
SPLITS = (ATTN_WIDTH, 2 * ATTN_WIDTH, 3 * ATTN_WIDTH, 3 * ATTN_WIDTH + ATTN_HEADS,
          4 * ATTN_WIDTH + ATTN_HEADS, 4 * ATTN_WIDTH + ATTN_HEADS + LRU_WIDTH)

kernel_name = "hymba_fox_rglru_parallel_heads"

def _rmsnorm(x, g):
    x32 = x.astype(jnp.float32)
    y = x32 * lax.rsqrt(jnp.mean(x32 * x32, axis=-1, keepdims=True) + NORM_EPS)
    return (y * g.astype(jnp.float32)).astype(x.dtype)

def _forgetting_attention(q, k, v, log_f):
    B, S, H, Dh = q.shape
    qh = q.transpose(0, 2, 1, 3)
    kh = k.transpose(0, 2, 1, 3)
    vh = v.transpose(0, 2, 1, 3)
    c = jnp.cumsum(log_f, axis=1).transpose(0, 2, 1)
    kpos = jnp.arange(S)
    scale = ATTN_HEAD_DIM ** -0.5
    n_blocks = S // Q_BLOCK

    def block(i):
        start = i * Q_BLOCK
        qb = lax.dynamic_slice_in_dim(qh, start, Q_BLOCK, axis=2)
        cq = lax.dynamic_slice_in_dim(c, start, Q_BLOCK, axis=2)
        s = jnp.einsum('bhqd,bhkd->bhqk', qb, kh,
                       preferred_element_type=jnp.float32) * scale
        s = s + cq[..., :, None] - c[..., None, :]
        qpos = start + jnp.arange(Q_BLOCK)
        s = jnp.where(kpos[None, :] <= qpos[:, None], s, -jnp.inf)
        p = jax.nn.softmax(s, axis=-1)
        return jnp.einsum('bhqk,bhkd->bhqd', p.astype(vh.dtype), vh)

    out = lax.map(block, jnp.arange(n_blocks))
    return out.transpose(1, 0, 3, 2, 4).reshape(B, S, H * Dh)

def _causal_depthwise_conv(x, w, b):
    y = lax.conv_general_dilated(
        x, w[:, None, :].astype(x.dtype), window_strides=(1,),
        padding=[(CONV_W - 1, 0)], dimension_numbers=('NWC', 'WIO', 'NWC'),
        feature_group_count=x.shape[-1])
    return y + b.astype(x.dtype)

def _rg_lru(x, w_r, b_r, w_i, b_i, lam):
    B, S, C = x.shape
    xb = x.reshape(B, S, LRU_BLOCKS, LRU_BLOCK_W)
    r = jax.nn.sigmoid((jnp.einsum('bsnc,ncd->bsnd', xb, w_r).reshape(B, S, C) + b_r).astype(jnp.float32))
    i = jax.nn.sigmoid((jnp.einsum('bsnc,ncd->bsnd', xb, w_i).reshape(B, S, C) + b_i).astype(jnp.float32))
    log_a = -LRU_C * r * jax.nn.softplus(-lam.astype(jnp.float32))
    a = jnp.exp(log_a)
    mult = jnp.sqrt(-jnp.expm1(2.0 * log_a))
    u = mult * i * x.astype(jnp.float32)

    def combine(left, right):
        a1, b1 = left
        a2, b2 = right
        return a1 * a2, a2 * b1 + b2

    _, h = lax.associative_scan(combine, (a, u), axis=1)
    return h.astype(x.dtype)

def setup_inputs(seed: int = 0) -> dict:
    key = jax.random.key(seed)
    ks = jax.random.split(key, 16)
    f32 = jnp.float32
    x = jax.random.normal(ks[0], (BATCH, SEQ, D_MODEL), f32)
    norm_g = 1.0 + 0.01 * jax.random.normal(ks[1], (DEPTH, D_MODEL), f32)
    w_in = jax.random.normal(ks[2], (DEPTH, D_MODEL, N_IN), f32) * D_MODEL ** -0.5
    b_f = 2.0 + 0.5 * jax.random.normal(ks[3], (DEPTH, ATTN_HEADS), f32)
    conv_w = jax.random.normal(ks[4], (DEPTH, CONV_W, LRU_WIDTH), f32) * CONV_W ** -0.5
    conv_b = 0.01 * jax.random.normal(ks[5], (DEPTH, LRU_WIDTH), f32)
    w_rg = jax.random.normal(ks[6], (DEPTH, LRU_BLOCKS, LRU_BLOCK_W, LRU_BLOCK_W), f32) * LRU_BLOCK_W ** -0.5
    b_rg = 0.01 * jax.random.normal(ks[7], (DEPTH, LRU_WIDTH), f32)
    w_ig = jax.random.normal(ks[8], (DEPTH, LRU_BLOCKS, LRU_BLOCK_W, LRU_BLOCK_W), f32) * LRU_BLOCK_W ** -0.5
    b_ig = 0.01 * jax.random.normal(ks[9], (DEPTH, LRU_WIDTH), f32)
    a0 = jax.random.uniform(ks[10], (DEPTH, LRU_WIDTH), f32, minval=0.9, maxval=0.999)
    lru_lambda = jnp.log(a0) - jnp.log1p(-a0)
    attn_norm_g = 1.0 + 0.01 * jax.random.normal(ks[11], (DEPTH, ATTN_WIDTH), f32)
    lru_norm_g = 1.0 + 0.01 * jax.random.normal(ks[12], (DEPTH, LRU_WIDTH), f32)
    w_out = jax.random.normal(ks[13], (DEPTH, D_MIX, D_MODEL), f32) * D_MIX ** -0.5
    final_norm_g = 1.0 + 0.01 * jax.random.normal(ks[14], (D_MODEL,), f32)
    return {"x": x, "norm_g": norm_g, "w_in": w_in, "b_f": b_f, "conv_w": conv_w,
            "conv_b": conv_b, "w_rg": w_rg, "b_rg": b_rg, "w_ig": w_ig, "b_ig": b_ig,
            "lru_lambda": lru_lambda, "attn_norm_g": attn_norm_g, "lru_norm_g": lru_norm_g,
            "w_out": w_out, "final_norm_g": final_norm_g}

def reference(x, norm_g, w_in, b_f, conv_w, conv_b, w_rg, b_rg, w_ig, b_ig,
              lru_lambda, attn_norm_g, lru_norm_g, w_out, final_norm_g):
    B, S, _ = x.shape
    for l in range(DEPTH):
        h = _rmsnorm(x, norm_g[l])
        proj = jnp.einsum('bsd,dn->bsn', h, w_in[l])
        q, k, v, f_logit, z_attn, x_lru, z_lru = jnp.split(proj, SPLITS, axis=-1)
        log_f = jax.nn.log_sigmoid((f_logit + b_f[l]).astype(jnp.float32))
        attn = _forgetting_attention(q.reshape(B, S, ATTN_HEADS, ATTN_HEAD_DIM),
                                     k.reshape(B, S, ATTN_HEADS, ATTN_HEAD_DIM),
                                     v.reshape(B, S, ATTN_HEADS, ATTN_HEAD_DIM), log_f)
        attn = _rmsnorm(attn, attn_norm_g[l]) * jax.nn.silu(z_attn)
        u = _causal_depthwise_conv(x_lru, conv_w[l], conv_b[l])
        lru = _rg_lru(u, w_rg[l], b_rg[l], w_ig[l], b_ig[l], lru_lambda[l])
        lru = _rmsnorm(lru, lru_norm_g[l]) * jax.nn.silu(z_lru)
        mixed = jnp.concatenate([attn, lru], axis=-1)
        x = x + jnp.einsum('bsm,md->bsd', mixed, w_out[l])
    return _rmsnorm(x, final_norm_g)


_drawn_inputs = setup_inputs


def setup_inputs(seed=0):
    import zlib

    import numpy as np

    out = dict(_drawn_inputs(seed))
    spreads = {}
    factors = {'norm_g': 6.482,
     'conv_b': 16.832,
     'b_rg': 60.085,
     'b_ig': 54.901,
     'attn_norm_g': 64.0,
     'lru_norm_g': 64.0,
     'final_norm_g': 31.045}
    for name, (base, spread) in spreads.items():
        noise = np.random.default_rng([zlib.crc32(name.encode()), seed]).standard_normal(out[name].shape)
        drawn = base * np.exp(spread * noise) if base else spread * noise
        out[name] = __import__('jax').numpy.asarray(drawn.astype(out[name].dtype))
    for name, factor in factors.items():
        out[name] = (out[name] * factor).astype(out[name].dtype)
    return out
```

```python
import concourse.bass as bass
from concourse import mybir
from contextlib import ExitStack

F32 = mybir.dt.float32
F32R = mybir.dt.float32r
ALU = mybir.AluOpType
ACT = mybir.ActivationFunctionType
AX_X = mybir.AxisListType.X
ds = bass.ds

P = 128
S = 512
TT = S // P
D = 2048
KC = D // P
W = D // 2
NH = W // P
EPS = 1e-6
SCALE = float(P) ** -0.5
LRU_C = 8.0
MASKED = -3.0e38

COL_Q, COL_K, COL_V = 0, W, 2 * W
COL_ZA = 3 * W + NH
COL_X = 4 * W + NH
COL_ZL = 5 * W + NH

RING = 4
CREDIT = RING
UCOLS = 1024
AHEAD = 3
VF = W + NH
A_GROUPS = 3
A_COLS = VF // A_GROUPS
A_FIRST = COL_V + (A_GROUPS - 1) * A_COLS
A_UNITS = 8
ROUNDS = 4
SLABS = 5
B_COLS = 2 * P
B_UNITS = 4
SLOTS = SLABS * B_UNITS
QUARTERS = 4
C_COLS = D // QUARTERS
C_UNITS = 8
N_A = A_GROUPS * A_UNITS
N_B = ROUNDS * SLOTS
N_C = QUARTERS * C_UNITS
B0 = N_A
C0 = N_A + N_B

TRI = [0, 128, 384, 768]
TRI_COLS = 1280
PT_AT = [0, 512, 1024, 896]
ATANH = [1.0 / 15, 1.0 / 13, 1.0 / 11, 1.0 / 9, 1.0 / 7, 1.0 / 5, 1.0 / 3]

V_CONVB, V_BR, V_BI, V_LAM, V_GA, V_GL, V_CONVW = range(7)
N_VEC = 10


def hybrid_layer(nc, x, norm_g, w_in, b_f, conv_w, conv_b, w_rg, b_rg, w_ig, b_ig, lru_lambda,
                 attn_norm_g, lru_norm_g, w_out, final_norm_g, out):
    w_in2 = w_in[0]
    w_out2 = w_out[0]
    x_tiles = x[0].rearrange("(t p) d -> t p d", p=P)
    out_tiles = out[0].rearrange("(t p) d -> t p d", p=P)

    with ExitStack() as ctx:
        here = [-(-nc.sbuf_base // 32) * 32]

        def region(nbytes):
            at = here[0]
            here[0] += nbytes
            assert here[0] <= nc.sbuf_usable_end, here[0]
            return at

        def sb(name, shape, at, dt=F32):
            return nc.alloc_sbuf_tensor_at(name, shape, dt, offset=at, align_bytes=4)

        def own(name, shape, dt=F32):
            n = 4
            for s in shape[1:]:
                n *= s
            return sb(name, shape, region(n), dt)

        def sem(name):
            return ctx.enter_context(nc.semaphore(name))

        hT_hi = own("hT_hi", [P, KC, S], F32R)
        hT_lo = own("hT_lo", [P, KC, S], F32R)
        raw = own("raw_ring", [P, RING, UCOLS])
        w_hi = own("w_hi_ring", [P, RING, UCOLS], F32R)
        w_lo = own("w_lo_ring", [P, RING, UCOLS], F32R)
        at_mix = region(4 * KC * S)
        x_in = sb("x_in", [P, TT, D], at_mix)
        mix = sb("mix", [P, KC, S], at_mix)
        y = sb("y", [P, TT, D], at_mix)
        at_v = region(4 * TT * VF)
        v_raw = sb("v_raw", [P, TT, VF], at_v)
        gain_out = sb("gain_out", [P, D], at_v)
        at_kq = region(8 * 4 * S)
        k_hi = sb("k_hi", [P, 2, S], at_kq, F32R)
        k_lo = sb("k_lo", [P, 2, S], at_kq + 4096, F32R)
        q_hi = sb("q_hi", [P, 2, S], at_kq + 8192, F32R)
        q_lo = sb("q_lo", [P, 2, S], at_kq + 12288, F32R)
        u_conv = sb("u_conv", [P, 2, S], at_kq)
        r_gate = sb("r_gate", [P, 2, S], at_kq + 4096)
        i_gate = sb("i_gate", [P, 2, S], at_kq + 8192)
        decay = sb("decay", [P, 2, S], at_kq + 12288)
        gain_in = sb("gain_in", [P, D], at_kq)
        at_probs = region(2 * 4 * TRI_COLS)
        probs = sb("probs", [P, 2, TRI_COLS], at_probs)
        junk = sb("junk", [P, D], at_probs)
        pT_hi = own("pT_hi", [P, TRI_COLS], F32R)
        pT_lo = own("pT_lo", [P, TRI_COLS], F32R)
        vh_hi = own("vh_hi", [P, TT, P], F32R)
        vh_lo = own("vh_lo", [P, TT, P], F32R)
        gate_w = own("gate_w", [P, 4, P])
        neg_c = own("neg_c", [NH, S])
        neg_c_head = own("neg_c_head", [P, 2, S])
        neg_c_dram = nc.dram_tensor("neg_c_dram", (NH, S), F32, kind="Internal").ap()
        squares = own("squares", [P, 2, S])
        sum_sq = own("sum_sq", [P, 2, S])
        z_sig = own("z_sig", [P, 2, S])
        ident = own("ident", [P, P])
        param = own("param", [P, N_VEC * NH])
        param_row = sb("param_row", [N_VEC * NH, P], at_probs + 4 * D)
        neg_ident = own("neg_ident", [NH, NH])
        ones_col = own("ones_col", [P, 1])
        bf_all = own("bf_all", [P, NH])
        SPC = TT * NH + NH
        sp_in, sp_e, sp_s, sp_s2, sp_q = (
            sb(name, [P, SPC], at_probs + 4 * D + 4 * P + 4 * SPC * i)
            for i, name in enumerate(("sp_in", "sp_e", "sp_s", "sp_s2", "sp_q")))
        softp = own("softp", [P, SPC])
        s8 = own("s8", [P, NH])
        neg_s8 = own("neg_s8", [P, NH])
        ms_x = own("ms_x", [P, TT])
        rstd_x = own("rstd_x", [P, TT])
        cq = own("cq", [P, 2, TT])
        row_max = own("row_max", [P, 2, TT])
        row_sum = own("row_sum", [P, 2, TT])
        row_inv = own("row_inv", [P, 2, TT])
        rstd_g = own("rstd_g", [P, 2 * TT])
        ms_y = own("ms_y", [P, TT, QUARTERS])
        rstd_y = own("rstd_y", [P, TT])

        bank = ctx.enter_context(nc.psum_tensor("bank", [P, 8, S], F32))

        x_loaded = [sem(f"x_loaded{t}") for t in range(TT)]
        gain_loaded = sem("gain_loaded")
        params_loaded = sem("params_loaded")
        raw_loaded = [sem(f"raw_loaded{s}") for s in range(RING)]
        gate_w_loaded = sem("gate_w_loaded")
        y_loaded = sem("y_loaded")
        gout_loaded = sem("gout_loaded")
        stored = sem("stored")
        consts_ready = sem("consts_ready")
        ident_zero = sem("ident_zero")
        x_squared = sem("x_squared")
        x_var = sem("x_var")
        x_std = sem("x_std")
        xn_ready = sem("xn_ready")
        x_turned = sem("x_turned")
        h_hi_ready = sem("h_hi_ready")
        h_lo_ready = sem("h_lo_ready")
        params_turned = sem("params_turned")
        param_ready = sem("param_ready")
        hi_ready = sem("hi_ready")
        lo_ready = sem("lo_ready")
        unit_used = sem("unit_used")
        v_done = sem("v_done")
        v_copied_act = sem("v_copied_act")
        v_copied_dve = sem("v_copied_dve")
        sp_neg = sem("sp_neg")
        sp_exp = sem("sp_exp")
        sp_ready = sem("sp_ready")
        sp_turned = sem("sp_turned")
        kq_hi_ready = sem("kq_hi_ready")
        kq_ready = sem("kq_ready")
        neg_c_ready = sem("neg_c_ready")
        neg_c_stored = sem("neg_c_stored")
        neg_c_loaded = [sem("neg_c_loaded0"), sem("neg_c_loaded1")]
        scores_done = sem("scores_done")
        cq_copied = sem("cq_copied")
        score_read = sem("score_read")
        biased = sem("biased")
        masked = sem("masked")
        row_maxed = sem("row_maxed")
        max_ready = sem("max_ready")
        exp_done = sem("exp_done")
        inv_ready = sem("inv_ready")
        probs_ready = sem("probs_ready")
        probs_turned = sem("probs_turned")
        pT_hi_ready = sem("pT_hi_ready")
        pT_ready = sem("pT_ready")
        vh_hi_ready = sem("vh_hi_ready")
        vh_ready = sem("vh_ready")
        pv_done = sem("pv_done")
        pv_read = sem("pv_read")
        squared = sem("squared")
        sq_added = sem("sq_added")
        u_begun = sem("u_begun")
        taps = sem("taps")
        u_ready = sem("u_ready")
        gates_done = sem("gates_done")
        gates_read = sem("gates_read")
        iu_ready = sem("iu_ready")
        zl_sig = sem("zl_sig")
        zl_read = sem("zl_read")
        act_lru = sem("act_lru")
        decay_ready = sem("decay_ready")
        mult_sq = sem("mult_sq")
        mult_ready = sem("mult_ready")
        drive_ready = sem("drive_ready")
        h_ready = sem("h_ready")
        h_squared = sem("h_squared")
        lru_done = sem("lru_done")
        za_sig = sem("za_sig")
        za_read = sem("za_read")
        mixA_done = sem("mixA_done")
        mix_hi_ready = sem("mix_hi_ready")
        mix_ready = sem("mix_ready")
        ssq_done = sem("ssq_done")
        g_var = sem("g_var")
        g_std = sem("g_std")
        g_rstd = sem("g_rstd")
        y_done = sem("y_done")
        y_read = sem("y_read")
        y_squared = sem("y_squared")
        y_gained = sem("y_gained")
        y_var = sem("y_var")
        y_std = sem("y_std")
        y_final = sem("y_final")
        dve_step = sem("dve_step")
        waits_passed = [sem("pool_waits_passed"), sem("sp_waits_passed")]

        def wait_alone(engine, semaphore, value):
            engine.wait_ge(semaphore, value).then_inc(waits_passed[engine is nc.sync], 1)

        KIND_A, KIND_B, KIND_C = (2, A_COLS), (KC // B_UNITS, B_COLS), (2, C_COLS)

        def slot(t, s, kind):
            return t[:, s, 0:kind[0] * kind[1]].rearrange("p (k n) -> p k n", k=kind[0])

        block = ctx.enter_context(nc.Block())

        @block.sync
        def _(sp):
            sp.dma_start(x_in[:, 0, :], x_tiles[0]).then_inc(x_loaded[0], 16)
            sp.dma_start(gain_in[:], norm_g[0].partition_broadcast(P)).then_inc(gain_loaded, 16)

            def fetch(s, kind, weights, row, col):
                rows = kind[0] * P
                sp.dma_start(slot(raw, s, kind), weights[row:row + rows, ds(col, kind[1])].rearrange(
                    "(k p) n -> p k n", p=P)).then_inc(raw_loaded[s], 16)

            for t in range(1, TT):
                if t == TT - 1:
                    for u in range(RING - 1):
                        fetch(u, KIND_A, w_in2, 2 * P * u, A_FIRST)
                sp.dma_start(x_in[:, t, :], x_tiles[t]).then_inc(x_loaded[t], 16)
            fetch(RING - 1, KIND_A, w_in2, 2 * P * (RING - 1), A_FIRST)

            def load(n, s, kind, weights, row, col):
                wait_alone(sp, lo_ready, n + 1)
                fetch(s, kind, weights, row, col)

            for u in range(RING, A_UNITS):
                load(u, u % RING, KIND_A, w_in2, 2 * P * u, A_FIRST)
            with sp.Fori(1, A_GROUPS) as g:
                for u in range(A_UNITS):
                    load(g * A_UNITS + u, u % RING, KIND_A, w_in2, 2 * P * u,
                         A_FIRST - g * A_COLS)
            with sp.Fori(0, ROUNDS) as g:
                for s, col in enumerate((COL_K, COL_Q, COL_X, COL_ZL, COL_ZA)):
                    for u in range(B_UNITS):
                        load(g * SLOTS + (B0 + s * B_UNITS + u), u % RING, KIND_B,
                             w_in2, 4 * P * u, g * B_COLS + col)
                    if s == 1:
                        wait_alone(sp, gates_done, g * 2 + 1)
                        sp.dma_start(gate_w[:, 0:2, :], w_rg[0][ds(g * 2, 2)].rearrange("b c d -> c b d")
                                     ).then_inc(gate_w_loaded, 16)
                        sp.dma_start(gate_w[:, 2:4, :], w_ig[0][ds(g * 2, 2)].rearrange("b c d -> c b d")
                                     ).then_inc(gate_w_loaded, 16)
            with sp.Fori(0, QUARTERS) as q:
                for u in range(C_UNITS):
                    load(q * C_UNITS + (C0 + u), u % RING, KIND_C,
                         w_out2, 2 * P * u, q * C_COLS)
            for t in range(TT):
                for part, cols in enumerate((slice(0, D - C_COLS), slice(D - C_COLS, D))):
                    sp.wait_ge(y_final, 2 * t + part + 1)
                    sp.dma_start(out_tiles[t][:, cols], y[:, t, cols]).then_inc(stored, 16)
            sp.wait_ge(stored, 2 * 16 * TT)

        @block.tensor
        def _(pe):
            def three(dst, a_hi, a_lo, b_hi, b_lo, start, stop):
                nc.tensor.matmul(dst, a_hi, b_hi, start=start, stop=False)
                nc.tensor.matmul(dst, a_hi, b_lo, start=False, stop=False)
                return nc.tensor.matmul(dst, a_lo, b_hi, start=False, stop=stop)

            pe.sem_inc(gates_done, 1)

            def turn_x(t):
                pe.wait_ge(xn_ready, t + 1)
                for b in range(4):
                    if t >= 1:
                        pe.wait_ge(h_lo_ready, 4 * (t - 1) + b + 1)
                    for j in range(4):
                        k = 4 * b + j
                        mm = nc.tensor.transpose(bank[:, 4 + b, j * P:(j + 1) * P],
                                                 x_in[:, t, k * P:(k + 1) * P], ident[:])
                    mm.then_inc(x_turned, 1)

            def wide(dst, k, t, s, kk, kind, start, stop):
                tok = slice(t * P, (t + 1) * P)
                return three(dst, hT_hi[:, k, tok], hT_lo[:, k, tok], slot(w_hi, s, kind)[:, kk, :],
                             slot(w_lo, s, kind)[:, kk, :], start, stop)

            pe.wait_ge(consts_ready, 1)
            turn_x(0)
            turn_x(1)
            for half in range(2):
                for t in range(TT):
                    if half == 0:
                        pe.wait_ge(h_lo_ready, 4 * (t + 1))
                    for u in range(4 * half, 4 * half + 4):
                        pe.wait_ge(lo_ready, u + 1 + CREDIT)
                        for kk in range(2):
                            k = 2 * u + kk
                            mm = wide(bank[:, t, 0:A_COLS], k, t, u % RING, kk, KIND_A, k == 0, k == KC - 1)
                            if k == KC - 1 and t < TT - 1:
                                mm.then_inc(v_done, 1)
                        if t == TT - 1:
                            mm.then_inc(unit_used, 1)
                    if half == 0 and t < TT - 2:
                        turn_x(t + 2)
                    if half == 0 and t == TT - 1:
                        pe.wait_ge(params_loaded, 16 * 8)
                        nc.tensor.transpose(bank[:, 4, 0:N_VEC * NH], param_row[:, :],
                                            ident[0:N_VEC * NH, 0:N_VEC * NH]).then_inc(params_turned, 1)

            with pe.Fori(1, A_GROUPS) as g:
                for u in range(A_UNITS):
                    pe.wait_ge(lo_ready, g * A_UNITS + (u + 1 + CREDIT))
                    for kk in range(2):
                        k = 2 * u + kk
                        for t in range(TT):
                            if k == 0:
                                pe.wait_ge((v_copied_act, v_copied_dve)[t % 2], g * 2 + (t // 2 - 1))
                            mm = wide(bank[:, t, 0:A_COLS], k, t, u % RING, kk, KIND_A, k == 0, k == KC - 1)
                            if k == KC - 1 and t < TT - 1:
                                mm.then_inc(v_done, 1)
                    mm.then_inc(unit_used, 1)
            pe.wait_ge(sp_ready, 1)
            for t in range(TT):
                mm = nc.tensor.transpose(bank[0:NH, 7, t * P:(t + 1) * P], softp[:, t * NH:(t + 1) * NH],
                                         ident[:])
            mm.then_inc(sp_turned, 1)
            pe.wait_ge(v_copied_act, 2 * A_GROUPS)
            pe.wait_ge(v_copied_dve, 2 * A_GROUPS)

            def unit(g, u, b0):
                pe.wait_ge(lo_ready, g * SLOTS + (B0 + u + 1 + CREDIT))
                hi, lo = slot(w_hi, u % RING, KIND_B), slot(w_lo, u % RING, KIND_B)
                for kk in range(4):
                    k = (u % B_UNITS) * 4 + kk
                    for c in range(2):
                        ch = slice(c * P, (c + 1) * P)
                        mm = three(bank[:, b0 + c, :], hi[:, kk, ch], lo[:, kk, ch], hT_hi[:, k, :],
                                   hT_lo[:, k, :], k == 0, k == KC - 1)
                mm.then_inc(unit_used, 1)

            def scores(g, c):
                if c == 0:
                    pe.wait_ge(za_read, g * 2 + 1)
                    pe.wait_ge(neg_c_ready, 1)
                pe.wait_ge(kq_ready, g * 4 + (3 + c))
                for i in range(TT):
                    if c == 1:
                        pe.wait_ge(score_read, g * 8 + (i + 1))
                    rows, keys = slice(i * P, (i + 1) * P), slice(0, (i + 1) * P)
                    mm = three(bank[:, 4 + i, keys], q_hi[:, c, rows], q_lo[:, c, rows], k_hi[:, c, keys],
                               k_lo[:, c, keys], True, True)
                    if i == 0:
                        for t in range(TT):
                            mm = nc.tensor.matmul(bank[:, 4, P + t:P + t + 1], neg_c[:, t * P:(t + 1) * P],
                                                  neg_ident[:, ds(g * 2 + c, 1)], start=True, stop=True)
                    mm.then_inc(scores_done, 1)

            def turn_probs(g, c):
                pe.wait_ge(probs_ready, g * 2 + (c + 1))
                if c == 0:
                    pe.wait_ge(score_read, g * 8 + 8)
                else:
                    pe.wait_ge(pT_ready, g * 6 + 3)
                for b, tiles in ((4, (0,)), (5, (1, 3)), (6, (2,))):
                    for j in tiles:
                        for i in range(j, TT):
                            at = PT_AT[j] - 512 * (b - 4) + (i - j) * P
                            mm = nc.tensor.transpose(bank[:, b, at:at + P],
                                                     probs[:, c, TRI[i] + j * P:TRI[i] + (j + 1) * P],
                                                     ident[:])
                    mm.then_inc(probs_turned, 1)

            def values(g, c):
                pe.wait_ge(pT_ready, g * 6 + 3 * (c + 1))
                pe.wait_ge(vh_ready, g * 2 + (c + 1))
                if c == 1:
                    pe.wait_ge(pv_read, g * 2 + 1)
                for j in range(TT):
                    cols = slice(PT_AT[j], PT_AT[j] + S - j * P)
                    mm = three(bank[:, 7, j * P:S], vh_hi[:, j, :], vh_lo[:, j, :], pT_hi[:, cols],
                               pT_lo[:, cols], j == 0, j == TT - 1)
                mm.then_inc(pv_done, 1)

            def gates(g, c):
                if c == 0:
                    pe.wait_ge(u_ready, g * 2 + 2)
                    pe.wait_ge(gate_w_loaded, g * 32 + 32)
                else:
                    pe.wait_ge(gates_read, g * 2 + 1)
                nc.tensor.matmul(bank[:, 0, :], gate_w[:, c, :], u_conv[:, c, :], start=True, stop=True)
                nc.tensor.matmul(bank[:, 1, :], gate_w[:, 2 + c, :], u_conv[:, c, :], start=True,
                                 stop=True).then_inc(gates_done, 1)

            with pe.Fori(0, ROUNDS) as g:
                for u in range(SLOTS):
                    if u in (9, 10):
                        scores(g, u - 9)
                    if u in (11, 13):
                        turn_probs(g, (u - 11) // 2)
                    if u in (12, 14):
                        values(g, (u - 12) // 2)
                    if u in (14, 15):
                        gates(g, u - 14)
                    if u == 18:
                        pe.wait_ge(gates_read, g * 2 + 2)
                    if u == 19:
                        pe.wait_ge(zl_read, g * 2 + 2)
                        pe.wait_ge(pv_read, g * 2 + 2)
                    unit(g, u, (0, 2, 0, 2, 4)[u // B_UNITS])

            pe.wait_ge(sq_added, 4 * ROUNDS)
            for i in range(2 * TT):
                mm = nc.tensor.matmul(bank[:, 6, i:i + 1], sum_sq[:, i // TT, (i % TT) * P:(i % TT + 1) * P],
                                      ones_col[:, :], start=True, stop=True)
            mm.then_inc(ssq_done, 1)
            pe.wait_ge(za_read, 2 * ROUNDS + 1)
            pe.wait_ge(g_var, 1)

            def project(q, units, tiles):
                for u in units:
                    pe.wait_ge(lo_ready, q * C_UNITS + (C0 + u + 1 + CREDIT))
                    pe.wait_ge(mix_ready, 2 * u + 2)
                    half = u // (C_UNITS // 2)
                    for kk in range(2):
                        k = 2 * u + kk
                        first, last = k % NH == 0, k % NH == NH - 1
                        for t in tiles:
                            if first:
                                pe.wait_ge(y_read, q * 8 + (4 * half + t + 1))
                            mm = wide(bank[:, 4 * half + t, :], k, t, u % RING, kk, KIND_C, first, last)
                            if last and t < TT - 1:
                                mm.then_inc(y_done, 1)
                    if TT - 1 in tiles:
                        mm.then_inc(unit_used, 1)

            with pe.Fori(0, QUARTERS - 1) as q:
                project(q, range(C_UNITS), range(TT))
            project(QUARTERS - 1, range(C_UNITS // 2), range(TT))
            for t in range(TT):
                project(QUARTERS - 1, range(C_UNITS // 2, C_UNITS), (t,))

        @block.scalar
        def _(act):
            def activate(dst, src, f, **kw):
                return nc.scalar.activation(dst, src, f, **kw)

            def split_hi(n, s, cols, loads):
                act.wait_ge(raw_loaded[s], loads * 16)
                act.wait_ge(unit_used, n + 1)
                activate(w_hi[:, s, 0:cols], raw[:, s, 0:cols], ACT.Copy).then_inc(hi_ready, 1)

            act.sem_inc(unit_used, RING)

            for row, (src, n) in enumerate(((conv_b[0], NH), (b_rg[0], NH), (b_ig[0], NH),
                                            (lru_lambda[0], NH), (attn_norm_g[0], NH),
                                            (lru_norm_g[0], NH))):
                act.dma_start(param_row[row * NH:row * NH + n, :], src.rearrange("(n p) -> n p", p=P)
                              ).then_inc(params_loaded, 16)
            act.dma_start(param_row[V_CONVW * NH:N_VEC * NH, :],
                          conv_w[0].rearrange("k (n p) -> (k n) p", p=P)).then_inc(params_loaded, 16)
            act.dma_start(bf_all[:], b_f[0].partition_broadcast(P)).then_inc(params_loaded, 16)

            def square_x(t):
                act.wait_ge(x_loaded[t], 16)
                if t >= 1:
                    act.wait_ge(x_squared, t)
                activate(junk[:], x_in[:, t, :], ACT.Square, accum_out=ms_x[:, t:t + 1]
                         ).then_inc(x_squared, 1)

            def std_x(t):
                act.wait_ge(x_var, t + 1)
                activate(rstd_x[:, t:t + 1], rstd_x[:, t:t + 1], ACT.Sqrt).then_inc(x_std, 1)

            def h_hi(t):
                for b in range(4):
                    act.wait_ge(x_turned, 4 * t + b + 1)
                    activate(hT_hi[:, 4 * b:4 * b + 4, t * P:(t + 1) * P],
                             bank[:, 4 + b, :].rearrange("p (k n) -> p k n", k=4), ACT.Copy).then_inc(h_hi_ready, 1)

            for t in range(TT):
                square_x(t)
                std_x(t)
                if t >= 1:
                    h_hi(t - 1)
                if 1 <= t <= 2:
                    split_hi(2 * t - 2, 2 * t - 2, 2 * A_COLS, 1)
                    split_hi(2 * t - 1, 2 * t - 1, 2 * A_COLS, 1)
            h_hi(TT - 1)

            def split_ahead(n):
                split_hi(n, n % RING, 2 * A_COLS if n < N_A else UCOLS, n // RING + 1)

            for g in range(A_GROUPS):
                for u in range(A_UNITS):
                    n = g * A_UNITS + u + AHEAD
                    if n >= RING:
                        split_ahead(n)
                    if g == 1 and u == 0:
                        act.wait_ge(sp_neg, 1)
                        activate(sp_e[:], sp_e[:], ACT.Exp).then_inc(sp_exp, 1)
                col = (A_GROUPS - 1 - g) * A_COLS
                for t in (0, 2):
                    act.wait_ge(v_done, 3 * g + t + 1)
                    activate(v_raw[:, t, col:col + A_COLS], bank[:, t, 0:A_COLS], ACT.Copy
                             ).then_inc(v_copied_act, 1)

            def split_round(g, u):
                n = B0 + u + AHEAD
                split_hi(g * SLOTS + n, n % RING, UCOLS, g * SLABS + (n // RING + 1))

            def to_hi(g, dst, b0, slot_end):
                act.wait_ge(unit_used, g * SLOTS + (B0 + slot_end + RING))
                for c in range(2):
                    activate(dst[:, c, :], bank[:, b0 + c, :], ACT.Copy).then_inc(kq_hi_ready, 1)

            def bias_scores(g, c):
                act.wait_ge(scores_done, g * 8 + (4 * c + 1))
                activate(cq[:, c, :], bank[:, 4, P:P + TT], ACT.Copy).then_inc(cq_copied, 1)
                act.wait_ge(cq_copied, g * 2 + (c + 1))
                for i in range(TT):
                    act.wait_ge(scores_done, g * 8 + (4 * c + i + 1))
                    activate(probs[:, c, TRI[i]:TRI[i] + (i + 1) * P], bank[:, 4 + i, 0:(i + 1) * P],
                             ACT.Identity, bias=cq[:, c, i:i + 1], scale=SCALE).then_inc(score_read, 1)

            def exp_scores(g, c):
                act.wait_ge(max_ready, g * 2 + (c + 1))
                for i in range(TT):
                    block_ = probs[:, c, TRI[i]:TRI[i] + (i + 1) * P]
                    activate(block_, block_, ACT.Exp, bias=row_max[:, c, i:i + 1],
                             accum_out=row_sum[:, c, i:i + 1]).then_inc(exp_done, 1)

            def pT_to_hi(g, c):
                for b, n in ((0, 512), (1, 512), (2, 256)):
                    act.wait_ge(probs_turned, g * 6 + (3 * c + b + 1))
                    activate(pT_hi[:, 512 * b:512 * b + n], bank[:, 4 + b, 0:n], ACT.Copy
                             ).then_inc(pT_hi_ready, 1)

            def head_v_hi(g, c):
                activate(vh_hi[:], v_raw[:, :, ds(g * 2 * P + c * P, P)], ACT.Copy
                         ).then_inc(vh_hi_ready, 1)

            def head_out(g, c):
                act.wait_ge(pv_done, g * 2 + (c + 1))
                activate(squares[:, c, :], bank[:, 7, :], ACT.Square).then_inc(squared, 1)
                activate(mix[:, ds(g * 2 + c, 1), :], bank[:, 7:8, :], ACT.Copy).then_inc(pv_read, 1)

            def column(vec, g, c):
                return param[:, ds(g * 2 + (vec * NH + c), 1)]

            act.wait_ge(neg_c_ready, 1)
            act.dma_start(neg_c_dram, neg_c[:]).then_inc(neg_c_stored, 16)
            act.wait_ge(neg_c_stored, 16)

            with act.Fori(0, ROUNDS) as g:
                for u in range(SLOTS):
                    split_round(g, u)
                    if u == 1:
                        for c in range(2):
                            act.dma_start(neg_c_head[:, c, :], neg_c_dram[ds(g * 2 + c, 1), :].rearrange(
                                "o s -> (o s)").partition_broadcast(P)).then_inc(neg_c_loaded[c], 16)
                    if u == 4:
                        to_hi(g, k_hi, 0, 4)
                    if u == 8:
                        to_hi(g, q_hi, 2, 8)
                    if u == 9:
                        head_v_hi(g, 0)
                        bias_scores(g, 0)
                    if u == 10:
                        exp_scores(g, 0)
                        bias_scores(g, 1)
                    if u == 11:
                        pT_to_hi(g, 0)
                        exp_scores(g, 1)
                    if u == 12:
                        act.wait_ge(unit_used, g * SLOTS + (B0 + 12 + RING))
                        for c in range(2):
                            activate(u_conv[:, c, :], bank[:, c, :], ACT.Identity,
                                     bias=column(V_CONVB, g, c), scale=column(V_CONVW + 3, g, c)
                                     ).then_inc(u_begun, 1)
                        head_out(g, 0)
                        head_v_hi(g, 1)
                    if u == 13:
                        pT_to_hi(g, 1)
                    if u == 14:
                        head_out(g, 1)
                    if u in (14, 15):
                        for c in (u - 14,):
                            act.wait_ge(gates_done, g * 2 + (c + 2))
                            activate(r_gate[:, c, :], bank[:, 0, :], ACT.Sigmoid, bias=column(V_BR, g, c)
                                     ).then_inc(act_lru, 1)
                            activate(i_gate[:, c, :], bank[:, 1, :], ACT.Sigmoid, bias=column(V_BI, g, c)
                                     ).then_inc(gates_read, 1)
                    if u == 16:
                        act.wait_ge(unit_used, g * SLOTS + (B0 + 16 + RING))
                        for c in range(2):
                            activate(z_sig[:, c, :], bank[:, 2 + c, :], ACT.Sigmoid).then_inc(zl_sig, 1)
                        act.wait_ge(act_lru, g * 2 + 2)
                        act.wait_ge(iu_ready, g * 2 + 2)
                        for c in range(2):
                            activate(decay[:, c, :], r_gate[:, c, :], ACT.Exp,
                                     scale=neg_s8[:, ds(g * 2 + c, 1)]).then_inc(decay_ready, 1)
                            activate(r_gate[:, c, :], r_gate[:, c, :], ACT.Tanh,
                                     scale=s8[:, ds(g * 2 + c, 1)])
                            act.wait_ge(decay_ready, g * 4 + (2 * c + 1))
                            activate(u_conv[:, c, :], decay[:, c, :], ACT.Square
                                     ).then_inc(decay_ready, 1)
                    if u == 17:
                        for c in range(2):
                            act.wait_ge(mult_sq, g * 2 + (c + 1))
                            activate(r_gate[:, c, :], r_gate[:, c, :], ACT.Sqrt).then_inc(mult_ready, 1)
                    if u == 18:
                        for c in range(2):
                            act.wait_ge(h_ready, g * 2 + (c + 1))
                            act.wait_ge(sq_added, g * 4 + (c + 1))
                            activate(squares[:, c:c + 1, :], mix[:, ds(g * 2 + (NH + c), 1), :],
                                     ACT.Square).then_inc(squared, 1)
                    if u == 19:
                        act.wait_ge(lru_done, g * 2 + 2)
                        act.wait_ge(sq_added, g * 4 + 4)
                        act.wait_ge(unit_used, g * SLOTS + (B0 + 20 + RING))
                        for c in range(2):
                            activate(z_sig[:, c, :], bank[:, 4 + c, :], ACT.Sigmoid).then_inc(za_sig, 1)

            def mix_hi(k):
                if k == 0:
                    act.wait_ge(mixA_done, 2 * ROUNDS)
                activate(hT_hi[:, k, :], mix[:, k, :], ACT.Copy).then_inc(mix_hi_ready, 1)

            for u in range(C_UNITS):
                split_ahead(C0 + u + AHEAD)
                if u < 4:
                    for k in range(4 * u, 4 * u + 4):
                        mix_hi(k)
                if u == 1:
                    act.wait_ge(g_var, 1)
                    activate(rstd_g[:], rstd_g[:], ACT.Sqrt).then_inc(g_std, 1)
                if u == 4:
                    act.wait_ge(mix_ready, KC)
                    act.dma_start(y[:], x[0].rearrange("(t p) d -> p t d", p=P)).then_inc(y_loaded, 16)
                    act.dma_start(gain_out[:], final_norm_g.partition_broadcast(P)).then_inc(gout_loaded, 16)

            def square_y(q, after=None):
                for t in range(TT):
                    act.wait_ge(y_read, q * 8 + (8 + 4 + t + 1))
                    activate(junk[:, t * C_COLS:(t + 1) * C_COLS], y[:, t, ds(q * C_COLS, C_COLS)], ACT.Square,
                             accum_out=ms_y[:, t, ds(q, 1)]).then_inc(y_squared, 1)
                    if after:
                        after(t)
                act.wait_ge(y_squared, q * TT + TT)

            with act.Fori(1, QUARTERS - 1) as q:
                for u in range(C_UNITS):
                    n = C0 + u + AHEAD
                    split_hi(q * C_UNITS + n, n % RING, UCOLS, q * 2 + (n // RING + 1))
                    if u == 1:
                        square_y(q - 1)
            q = QUARTERS - 1
            for u in range(C_UNITS - AHEAD):
                split_ahead(C0 + q * C_UNITS + u + AHEAD)
                if u == 1:
                    square_y(q - 1)

            def std_y(t):
                act.wait_ge(y_var, t + 1)
                activate(rstd_y[:, t:t + 1], rstd_y[:, t:t + 1], ACT.Sqrt).then_inc(y_std, 1)

            square_y(q, std_y)

        @block.gpsimd
        def _(pool):
            nc.gpsimd.memset(ident[:], 0.0).then_inc(ident_zero, 1)
            nc.gpsimd.memset(ones_col[:], 1.0)
            nc.gpsimd.memset(sum_sq[:], 0.0).then_inc(ident_zero, 1)
            pool.wait_ge(ident_zero, 2)
            nc.gpsimd.affine_select(out=ident[:], in_=ident[:], compare_op=ALU.not_equal, fill=1.0,
                                    base=0, pattern=[[-1, P]], channel_multiplier=1).then_inc(consts_ready, 1)
            for n in range(RING):
                pool.wait_ge(hi_ready, n + 1)
                nc.gpsimd.tensor_tensor(w_lo[:, n, 0:2 * A_COLS], raw[:, n, 0:2 * A_COLS],
                                        w_hi[:, n, 0:2 * A_COLS].bitcast(F32), ALU.subtract
                                        ).then_inc(lo_ready, 1)

            def mask(g, c):
                for i in range(TT):
                    wait_alone(pool, biased, g * 8 + (4 * c + i + 1))
                    at = TRI[i] + i * P
                    nc.gpsimd.affine_select(out=probs[:, c, at:at + P], in_=probs[:, c, at:at + P],
                                            compare_op=ALU.is_ge, fill=masked_fill, base=0,
                                            pattern=[[-1, P]], channel_multiplier=1).then_inc(masked, 1)

            def add_squares(g, group, c):
                pool.wait_ge(squared, g * 4 + (2 * group + c + 1))
                if c:
                    pool.wait_ge(sq_added, g * 4 + (2 * group + c))
                nc.gpsimd.tensor_tensor(sum_sq[:, group, :], sum_sq[:, group, :], squares[:, c, :],
                                        ALU.add).then_inc(sq_added, 1)

            masked_fill = nc.gpsimd.to_reg(MASKED)
            with pool.Fori(0, ROUNDS) as g:
                mask(g, 0)
                mask(g, 1)
                for group in range(2):
                    for c in range(2):
                        add_squares(g, group, c)
                pool.wait_ge(sq_added, g * 4 + 4)

            with pool.Fori(0, QUARTERS - 1) as q:
                pool.wait_ge(gout_loaded, 16)
                for t in range(TT):
                    pool.wait_ge(y_squared, q * TT + (t + 1))
                    chunk = y[:, t, ds(q * C_COLS, C_COLS)]
                    nc.gpsimd.tensor_tensor(chunk, chunk, gain_out[:, ds(q * C_COLS, C_COLS)], ALU.mult
                                            ).then_inc(y_gained, 1)

        @block.vector
        def _(dve):
            steps = [0]

            def step(ins):
                steps[0] += 1
                ins.then_inc(dve_step, 1)
                dve.wait_ge(dve_step, steps[0])

            def split_lo(n, s, cols):
                dve.wait_ge(hi_ready, n + 1)
                nc.vector.tensor_tensor(w_lo[:, s, 0:cols], raw[:, s, 0:cols], w_hi[:, s, 0:cols].bitcast(F32),
                                        ALU.subtract).then_inc(lo_ready, 1)

            def split_ahead(n):
                split_lo(n, n % RING, 2 * A_COLS if n < N_A else UCOLS)

            dve.sem_inc(lo_ready, CREDIT)
            dve.sem_inc(za_read, 1)
            dve.sem_inc(y_read, 8)

            def normalise(t):
                dve.wait_ge(x_squared, t + 1)
                nc.vector.tensor_scalar(rstd_x[:, t:t + 1], ms_x[:, t:t + 1], 1.0 / D, EPS, ALU.mult,
                                        ALU.add).then_inc(x_var, 1)
                dve.wait_ge(x_std, t + 1)
                step(nc.vector.reciprocal(rstd_x[:, t:t + 1], rstd_x[:, t:t + 1]))
                if t == 0:
                    dve.wait_ge(gain_loaded, 16)
                nc.vector.scalar_tensor_tensor(out=x_in[:, t, :], in0=x_in[:, t, :],
                                               scalar=rstd_x[:, t:t + 1], in1=gain_in[:], op0=ALU.mult,
                                               op1=ALU.mult).then_inc(xn_ready, 1)

            def h_lo(t):
                for b in range(4):
                    dve.wait_ge(h_hi_ready, 4 * t + b + 1)
                    out_ = (slice(None), slice(4 * b, 4 * b + 4), slice(t * P, (t + 1) * P))
                    nc.vector.tensor_tensor(hT_lo[out_], bank[:, 4 + b, :].rearrange(
                        "p (k n) -> p k n", k=4), hT_hi[out_].bitcast(F32), ALU.subtract).then_inc(h_lo_ready, 1)

            for t in range(TT):
                normalise(t)
                if t >= 1:
                    h_lo(t - 1)
            h_lo(TT - 1)
            dve.wait_ge(params_turned, 1)
            nc.vector.tensor_copy(param[:], bank[:, 4, 0:N_VEC * NH]).then_inc(param_ready, 1)

            dve.wait_ge(consts_ready, 1)
            nc.vector.tensor_scalar(neg_ident[:], ident[0:NH, 0:NH], -1.0, None, ALU.mult)

            def softplus_begin():
                dve.wait_ge(v_copied_act, 2)
                dve.wait_ge(v_copied_dve, 2)
                dve.wait_ge(param_ready, 1)
                for t in range(TT):
                    nc.vector.tensor_tensor(sp_in[:, t * NH:(t + 1) * NH], v_raw[:, t, W:W + NH], bf_all[:],
                                            ALU.add)
                step(nc.vector.tensor_copy(sp_in[:, TT * NH:SPC], param[:, V_LAM * NH:(V_LAM + 1) * NH]))
                nc.vector.scalar_tensor_tensor(out=sp_e[:], in0=sp_in[:], scalar=-1.0, in1=sp_in[:],
                                               op0=ALU.mult, op1=ALU.min).then_inc(sp_neg, 1)

            def softplus_end():
                dve.wait_ge(sp_exp, 1)
                step(nc.vector.tensor_scalar(sp_s[:], sp_e[:], 2.0, None, ALU.add))
                step(nc.vector.reciprocal(sp_s[:], sp_s[:]))
                step(nc.vector.tensor_tensor(sp_s[:], sp_s[:], sp_e[:], ALU.mult))
                step(nc.vector.tensor_tensor(sp_s2[:], sp_s[:], sp_s[:], ALU.mult))
                step(nc.vector.tensor_scalar(sp_q[:], sp_s2[:], ATANH[0], None, ALU.mult))
                for a in ATANH[1:]:
                    step(nc.vector.scalar_tensor_tensor(out=sp_q[:], in0=sp_q[:], scalar=a, in1=sp_s2[:],
                                                        op0=ALU.add, op1=ALU.mult))
                step(nc.vector.scalar_tensor_tensor(out=sp_q[:], in0=sp_q[:], scalar=1.0, in1=sp_s[:],
                                                    op0=ALU.add, op1=ALU.mult))
                step(nc.vector.tensor_scalar(sp_in[:], sp_in[:], -1.0, 0.0, ALU.mult, ALU.max))
                step(nc.vector.scalar_tensor_tensor(out=softp[:], in0=sp_q[:], scalar=2.0, in1=sp_in[:],
                                                    op0=ALU.mult, op1=ALU.add))
                nc.vector.tensor_scalar(s8[:], softp[:, TT * NH:SPC], LRU_C, None, ALU.mult)
                step(nc.vector.tensor_scalar(neg_s8[:], softp[:, TT * NH:SPC], -LRU_C, None, ALU.mult))
                dve.sem_inc(sp_ready, 1)

            for g in range(A_GROUPS):
                for u in range(A_UNITS):
                    n = g * A_UNITS + u + AHEAD
                    if n >= RING:
                        split_ahead(n)
                    if g == 1 and u == 0:
                        softplus_begin()
                    if g == 1 and u == 1:
                        softplus_end()
                col = (A_GROUPS - 1 - g) * A_COLS
                for t in (1, 3):
                    if t == 3:
                        dve.wait_ge(unit_used, (g + 1) * A_UNITS + RING)
                    else:
                        dve.wait_ge(v_done, 3 * g + t + 1)
                    nc.vector.tensor_copy(v_raw[:, t, col:col + A_COLS], bank[:, t, 0:A_COLS]
                                          ).then_inc(v_copied_dve, 1)
            dve.wait_ge(sp_turned, 1)
            step(nc.vector.memset(neg_c_head[0:NH, 0, :], 1.0))
            nc.vector.tensor_tensor_scan(neg_c[:], neg_c_head[0:NH, 0, :], bank[0:NH, 7, :], 0.0,
                                         ALU.mult, ALU.add).then_inc(neg_c_ready, 1)

            def to_lo(g, b0, hi, lo, first):
                for c in range(2):
                    dve.wait_ge(kq_hi_ready, g * 4 + (first + c + 1))
                    nc.vector.tensor_tensor(lo[:, c, :], bank[:, b0 + c, :], hi[:, c, :].bitcast(F32),
                                            ALU.subtract).then_inc(kq_ready, 1)

            def head_v_lo(g, c):
                dve.wait_ge(vh_hi_ready, g * 2 + (c + 1))
                nc.vector.tensor_tensor(vh_lo[:], v_raw[:, :, ds(g * 2 * P + c * P, P)],
                                        vh_hi[:].bitcast(F32), ALU.subtract).then_inc(vh_ready, 1)

            def bias_keys(g, c):
                dve.wait_ge(neg_c_loaded[c], g * 16 + 16)
                for i in range(TT):
                    dve.wait_ge(score_read, g * 8 + (4 * c + i + 1))
                    row = probs[:, c, TRI[i]:TRI[i] + (i + 1) * P]
                    nc.vector.tensor_tensor(row, row, neg_c_head[:, c, 0:(i + 1) * P], ALU.add
                                            ).then_inc(biased, 1)
                for i in range(TT):
                    dve.wait_ge(masked, g * 8 + (4 * c + i + 1))
                    nc.vector.reduce_max(row_sum[:, c, i:i + 1], probs[:, c, TRI[i]:TRI[i] + (i + 1) * P],
                                         AX_X).then_inc(row_maxed, 1)
                dve.wait_ge(row_maxed, g * 8 + (4 * c + 4))
                nc.vector.tensor_scalar(row_max[:, c, :], row_sum[:, c, :], -1.0, None, ALU.mult
                                        ).then_inc(max_ready, 1)

            def normalise_probs(g, c):
                dve.wait_ge(exp_done, g * 8 + (4 * c + 4))
                nc.vector.reciprocal(row_inv[:, c, :], row_sum[:, c, :]).then_inc(inv_ready, 1)
                dve.wait_ge(inv_ready, g * 2 + (c + 1))
                for i in range(TT):
                    row = probs[:, c, TRI[i]:TRI[i] + (i + 1) * P]
                    ins = nc.vector.tensor_scalar(row, row, row_inv[:, c, i:i + 1], None, ALU.mult)
                ins.then_inc(probs_ready, 1)

            def pT_to_lo(g, c):
                for b, n in ((0, 512), (1, 512), (2, 256)):
                    dve.wait_ge(pT_hi_ready, g * 6 + (3 * c + b + 1))
                    cols = slice(512 * b, 512 * b + n)
                    nc.vector.tensor_tensor(pT_lo[:, cols], bank[:, 4 + b, 0:n], pT_hi[:, cols].bitcast(F32),
                                            ALU.subtract).then_inc(pT_ready, 1)

            def column(vec, g, c):
                return param[:, ds(g * 2 + (vec * NH + c), 1)]

            def convolve(g):
                for back in range(1, 4):
                    for c in range(2):
                        if back == 1:
                            dve.wait_ge(u_begun, g * 2 + (c + 1))
                        else:
                            dve.wait_ge(taps, g * 4 + (2 * (back - 2) + c + 1))
                        nc.vector.scalar_tensor_tensor(
                            out=u_conv[:, c, back:S], in0=bank[:, c, 0:S - back],
                            scalar=column(V_CONVW + 3 - back, g, c), in1=u_conv[:, c, back:S],
                            op0=ALU.mult, op1=ALU.add).then_inc(u_ready if back == 3 else taps, 1)

            with dve.Fori(0, ROUNDS) as g:
                for u in range(SLOTS):
                    n = B0 + u + AHEAD
                    split_lo(g * SLOTS + n, n % RING, UCOLS)
                    if u == 4:
                        to_lo(g, 0, k_hi, k_lo, 0)
                    if u == 8:
                        to_lo(g, 2, q_hi, q_lo, 2)
                    if u == 9:
                        head_v_lo(g, 0)
                        bias_keys(g, 0)
                    if u == 10:
                        normalise_probs(g, 0)
                        bias_keys(g, 1)
                    if u == 11:
                        pT_to_lo(g, 0)
                        normalise_probs(g, 1)
                    if u == 12:
                        convolve(g)
                        head_v_lo(g, 1)
                    if u == 13:
                        pT_to_lo(g, 1)
                    if u == 15:
                        for c in range(2):
                            dve.wait_ge(gates_read, g * 2 + (c + 1))
                            nc.vector.tensor_tensor(i_gate[:, c, :], i_gate[:, c, :], u_conv[:, c, :],
                                                    ALU.mult).then_inc(iu_ready, 1)
                    if u == 16:
                        for c in range(2):
                            dve.wait_ge(zl_sig, g * 2 + (c + 1))
                            nc.vector.tensor_tensor(z_sig[:, c, :], bank[:, 2 + c, :], z_sig[:, c, :],
                                                    ALU.mult).then_inc(zl_read, 1)
                        for c in range(2):
                            dve.wait_ge(decay_ready, g * 4 + (2 * c + 2))
                            nc.vector.scalar_tensor_tensor(out=r_gate[:, c, :], in0=u_conv[:, c, :],
                                                           scalar=1.0, in1=r_gate[:, c, :], op0=ALU.add,
                                                           op1=ALU.mult).then_inc(mult_sq, 1)
                    if u == 17:
                        for c in range(2):
                            dve.wait_ge(mult_ready, g * 2 + (c + 1))
                            nc.vector.tensor_tensor(i_gate[:, c, :], i_gate[:, c, :], r_gate[:, c, :],
                                                    ALU.mult).then_inc(drive_ready, 1)
                        for c in range(2):
                            dve.wait_ge(drive_ready, g * 2 + (c + 1))
                            nc.vector.tensor_tensor_scan(mix[:, ds(g * 2 + (NH + c), 1), :].rearrange(
                                "p o s -> p (o s)"), decay[:, c, :], i_gate[:, c, :], 0.0, ALU.mult,
                                ALU.add).then_inc(h_ready, 1)
                    if u == 18:
                        for c in range(2):
                            dve.wait_ge(squared, g * 4 + (3 + c))
                            tile = mix[:, ds(g * 2 + (NH + c), 1), :]
                            nc.vector.scalar_tensor_tensor(out=tile, in0=tile, scalar=column(V_GL, g, c),
                                                           in1=z_sig[:, c:c + 1, :], op0=ALU.mult,
                                                           op1=ALU.mult).then_inc(lru_done, 1)
                    if u == 19:
                        for c in range(2):
                            dve.wait_ge(za_sig, g * 2 + (c + 1))
                            nc.vector.tensor_tensor(z_sig[:, c, :], bank[:, 4 + c, :], z_sig[:, c, :],
                                                    ALU.mult).then_inc(za_read, 1)
                        for c in range(2):
                            dve.wait_ge(za_read, g * 2 + (c + 2))
                            tile = mix[:, ds(g * 2 + c, 1), :]
                            nc.vector.scalar_tensor_tensor(out=tile, in0=tile, scalar=column(V_GA, g, c),
                                                           in1=z_sig[:, c:c + 1, :], op0=ALU.mult,
                                                           op1=ALU.mult).then_inc(mixA_done, 1)

            def mix_lo(k):
                dve.wait_ge(mix_hi_ready, k + 1)
                nc.vector.tensor_tensor(hT_lo[:, k, :], mix[:, k, :], hT_hi[:, k, :].bitcast(F32),
                                        ALU.subtract).then_inc(mix_ready, 1)

            def add_half(q, half, tiles=range(TT)):
                for t in tiles:
                    if t == TT - 1:
                        dve.wait_ge(unit_used, q * C_UNITS + (C0 + (half + 1) * C_UNITS // 2 + RING))
                    else:
                        dve.wait_ge(y_done, q * 6 + (3 * half + t + 1))
                    chunk = y[:, t, ds(q * C_COLS, C_COLS)]
                    if half == 1:
                        dve.wait_ge(y_read, q * 8 + (8 + t + 1))
                    nc.vector.scalar_tensor_tensor(out=chunk, in0=bank[:, 4 * half + t, :],
                                                   scalar=rstd_g[:, 4 * half + t:4 * half + t + 1],
                                                   in1=chunk, op0=ALU.mult, op1=ALU.add).then_inc(y_read, 1)

            for u in range(C_UNITS):
                split_ahead(C0 + u + AHEAD)
                if u == 0:
                    dve.wait_ge(ssq_done, 1)
                    nc.vector.tensor_scalar(rstd_g[:], bank[:, 6, 0:2 * TT], 1.0 / W, EPS, ALU.mult,
                                            ALU.add).then_inc(g_var, 1)
                if u < 4:
                    for k in range(4 * u, 4 * u + 4):
                        mix_lo(k)
                if u == 2:
                    dve.wait_ge(g_std, 1)
                    nc.vector.reciprocal(rstd_g[:], rstd_g[:]).then_inc(g_rstd, 1)
                if u == 5:
                    dve.wait_ge(g_rstd, 1)
                    dve.wait_ge(y_loaded, 16)
                    add_half(0, 0)
            add_half(0, 1)
            with dve.Fori(1, QUARTERS - 1) as q:
                for u in range(C_UNITS):
                    n = C0 + u + AHEAD
                    split_lo(q * C_UNITS + n, n % RING, UCOLS)
                    if u == 4:
                        add_half(q, 0)
                add_half(q, 1)
            q = QUARTERS - 1
            for u in range(C_UNITS - AHEAD):
                split_ahead(C0 + q * C_UNITS + u + AHEAD)
                if u == 4:
                    add_half(q, 0)
            dve.wait_ge(gout_loaded, 16)
            dve.wait_ge(y_gained, (QUARTERS - 1) * TT)
            first, last = slice(0, q * C_COLS), slice(q * C_COLS, D)
            for t in range(TT):
                add_half(q, 1, (t,))
                dve.wait_ge(y_squared, q * TT + t + 1)
                step(nc.vector.reduce_sum(rstd_y[:, t:t + 1], ms_y[:, t, :], AX_X))
                nc.vector.tensor_scalar(rstd_y[:, t:t + 1], rstd_y[:, t:t + 1], 1.0 / D, EPS, ALU.mult,
                                        ALU.add).then_inc(y_var, 1)
                dve.wait_ge(y_std, t + 1)
                step(nc.vector.reciprocal(rstd_y[:, t:t + 1], rstd_y[:, t:t + 1]))
                nc.vector.tensor_scalar(y[:, t, first], y[:, t, first], rstd_y[:, t:t + 1], None, ALU.mult
                                        ).then_inc(y_final, 1)
                nc.vector.scalar_tensor_tensor(out=y[:, t, last], in0=y[:, t, last],
                                               scalar=rstd_y[:, t:t + 1], in1=gain_out[:, last],
                                               op0=ALU.mult, op1=ALU.mult).then_inc(y_final, 1)


_INS = ['x', 'norm_g', 'w_in', 'b_f', 'conv_w', 'conv_b', 'w_rg', 'b_rg', 'w_ig', 'b_ig', 'lru_lambda',
        'attn_norm_g', 'lru_norm_g', 'w_out', 'final_norm_g']


def kernel(**inputs):
    import numpy as np
    import concourse.bacc as bacc
    from concourse.bass_utils import run_bass_kernel_spmd

    nc = bacc.Bacc("TRN2", target_bir_lowering=False, num_devices=1, dynamic_dma_scratch_size=1024)
    arrays, args = {}, []
    for name in _INS:
        a = np.ascontiguousarray(inputs[name])
        arrays[f"in_{name}_dram"] = a
        args.append(nc.dram_tensor(f"in_{name}_dram", a.shape, mybir.dt.from_np(a.dtype),
                                   kind="ExternalInput").ap())
    args.append(nc.dram_tensor("out_dram", inputs['x'].shape, F32, kind="ExternalOutput").ap())
    hybrid_layer(nc, *args)
    r = run_bass_kernel_spmd(nc, [arrays], core_ids=[0])
    return r.results[0]["out_dram"]
```

```python
import concourse.bass as bass
from concourse import mybir
from contextlib import ExitStack

F32 = mybir.dt.float32
F32R = mybir.dt.float32r
ALU = mybir.AluOpType
ACT = mybir.ActivationFunctionType
AX_X = mybir.AxisListType.X
ds = bass.ds

P = 128
S = 512
TT = S // P
D = 2048
KC = D // P
W = D // 2
NH = W // P
EPS = 1e-6
SCALE = float(P) ** -0.5
LRU_C = 8.0
MASKED = -3.0e38

COL_Q, COL_K, COL_V = 0, W, 2 * W
COL_ZA = 3 * W + NH
COL_X = 4 * W + NH
COL_ZL = 5 * W + NH

RING = 4
CREDIT = RING
UCOLS = 1024
AHEAD = 3
VF = W + NH
A_GROUPS = 3
A_COLS = VF // A_GROUPS
A_FIRST = COL_V + (A_GROUPS - 1) * A_COLS
A_UNITS = 8
ROUNDS = 4
SLABS = 5
B_COLS = 2 * P
B_UNITS = 4
SLOTS = SLABS * B_UNITS
QUARTERS = 4
C_COLS = D // QUARTERS
C_UNITS = 8
FIRST, MIDDLE, LAST = slice(0, 704), slice(704, D - C_COLS), slice(D - C_COLS, D)
N_A = A_GROUPS * A_UNITS
N_B = ROUNDS * SLOTS
B0 = N_A
C0 = N_A + N_B

TRI = [0, 128, 384, 768]
TRI_COLS = 1280
PT_AT = [0, 512, 1024, 896]
ATANH = [1.0 / 15, 1.0 / 13, 1.0 / 11, 1.0 / 9, 1.0 / 7, 1.0 / 5, 1.0 / 3]

V_CONVB, V_BR, V_BI, V_LAM, V_GA, V_GL, V_CONVW = range(7)
N_VEC = 10


def hybrid_layer(nc, x, norm_g, w_in, b_f, conv_w, conv_b, w_rg, b_rg, w_ig, b_ig, lru_lambda,
                 attn_norm_g, lru_norm_g, w_out, final_norm_g, out):
    w_in2 = w_in[0]
    w_out2 = w_out[0]
    x_tiles = x[0].rearrange("(t p) d -> t p d", p=P)
    out_tiles = out[0].rearrange("(t p) d -> t p d", p=P)

    with ExitStack() as ctx:
        here = [-(-nc.sbuf_base // 32) * 32]

        def region(nbytes):
            at = here[0]
            here[0] += nbytes
            assert here[0] <= nc.sbuf_usable_end, here[0]
            return at

        def sb(name, shape, at, dt=F32):
            return nc.alloc_sbuf_tensor_at(name, shape, dt, offset=at, align_bytes=4)

        def own(name, shape, dt=F32):
            n = 4
            for s in shape[1:]:
                n *= s
            return sb(name, shape, region(n), dt)

        def sem(name):
            return ctx.enter_context(nc.semaphore(name))

        hT_hi = own("hT_hi", [P, KC, S], F32R)
        hT_lo = own("hT_lo", [P, KC, S], F32R)
        raw = own("raw_ring", [P, RING, UCOLS])
        w_hi = own("w_hi_ring", [P, RING, UCOLS], F32R)
        w_lo = own("w_lo_ring", [P, RING, UCOLS], F32R)
        at_mix = region(4 * KC * S)
        x_in = sb("x_in", [P, TT, D], at_mix)
        mix = sb("mix", [P, KC, S], at_mix)
        y = sb("y", [P, TT, D], at_mix)
        at_v = region(4 * TT * VF)
        v_raw = sb("v_raw", [P, TT, VF], at_v)
        gain_out = sb("gain_out", [P, D], at_v)
        at_kq = region(8 * 4 * S)
        k_hi = sb("k_hi", [P, 2, S], at_kq, F32R)
        k_lo = sb("k_lo", [P, 2, S], at_kq + 4096, F32R)
        q_hi = sb("q_hi", [P, 2, S], at_kq + 8192, F32R)
        q_lo = sb("q_lo", [P, 2, S], at_kq + 12288, F32R)
        u_conv = sb("u_conv", [P, 2, S], at_kq)
        r_gate = sb("r_gate", [P, 2, S], at_kq + 4096)
        i_gate = sb("i_gate", [P, 2, S], at_kq + 8192)
        decay = sb("decay", [P, 2, S], at_kq + 12288)
        gain_in = sb("gain_in", [P, D], at_kq)
        at_probs = region(2 * 4 * TRI_COLS)
        probs = sb("probs", [P, 2, TRI_COLS], at_probs)
        junk = sb("junk", [P, D], at_probs)
        at_pT = region(8 * TRI_COLS)
        pT_hi = sb("pT_hi", [P, TRI_COLS], at_pT, F32R)
        pT_lo = sb("pT_lo", [P, TRI_COLS], at_pT + 4 * TRI_COLS, F32R)
        first_hi = sb("first_hi", [P, 2, S], at_pT, F32R)
        first_lo = sb("first_lo", [P, 2, S], at_pT + 4 * TRI_COLS, F32R)
        at_vh = region(4 * TT * P)
        vh_hi = sb("vh_hi", [P, TT, P], at_vh, F32R)
        vh_lo = own("vh_lo", [P, TT, P], F32R)
        gate_w = own("gate_w", [P, 4, P])
        neg_c = own("neg_c", [NH, S])
        at_neg_c = region(8 * S)
        neg_c_head = sb("neg_c_head", [P, 2, S], at_neg_c)
        gate_hi = sb("gate_hi", [P, 4, P], at_neg_c, F32R)
        gate_lo = sb("gate_lo", [P, 4, P], at_neg_c + 16 * P, F32R)
        neg_c_dram = nc.dram_tensor("neg_c_dram", (NH, S), F32, kind="Internal").ap()
        squares = own("squares", [P, 2, S])
        sum_sq = own("sum_sq", [P, 2, S])
        at_z = region(8 * S)
        z_sig = sb("z_sig", [P, 2, S], at_z)
        u_hi = sb("u_hi", [P, 2, S], at_kq + 12288, F32R)
        u_lo = sb("u_lo", [P, 2, S], at_z, F32R)
        ident = own("ident", [P, P])
        param = own("param", [P, N_VEC * NH])
        param_row = sb("param_row", [N_VEC * NH, P], at_probs + 4 * D)
        upper = sb("upper", [P, P], at_probs + 2 * 4 * TRI_COLS - 4 * P)
        ones = sb("ones", [P, P], at_vh)
        ones_row = sb("ones_row", [1, P], at_v + 4 * D, F32R)
        gain_row = sb("gain_row", [1, D], at_v)
        gain_hi = sb("gain_hi", [1, D], at_kq + 4 * D, F32R)
        gain_lo = sb("gain_lo", [1, D], at_pT, F32R)
        ms_x0 = own("ms_x0", [P, 1])
        ones_col = own("ones_col", [P, 1])
        bf_all = own("bf_all", [P, NH])
        SPC = TT * NH + NH
        sp_in, sp_e, sp_s, sp_s2, sp_q = (
            sb(name, [P, SPC], at_probs + 4 * D + 4 * P + 4 * SPC * i)
            for i, name in enumerate(("sp_in", "sp_e", "sp_s", "sp_s2", "sp_q")))
        softp = own("softp", [P, SPC])
        s8 = own("s8", [P, NH])
        neg_s8 = own("neg_s8", [P, NH])
        ms_x = own("ms_x", [P, TT])
        rstd_x = own("rstd_x", [P, TT])
        cq = own("cq", [P, TT, NH])
        row_max = own("row_max", [P, 2, TT])
        row_sum = own("row_sum", [P, 2, TT])
        row_inv = own("row_inv", [P, 2, TT])
        rstd_g = own("rstd_g", [P, 2 * TT])
        ms_y = own("ms_y", [P, TT, QUARTERS])
        rstd_y = own("rstd_y", [P, TT])
        ms_first = own("ms_first", [P, TT])

        bank = ctx.enter_context(nc.psum_tensor("bank", [P, 8, S], F32))

        x_loaded = [sem(f"x_loaded{t}") for t in range(TT)]
        x_half_loaded = sem("x_half_loaded")
        x_half_squared = sem("x_half_squared")
        table_loaded = sem("table_loaded")
        gain_loaded = sem("gain_loaded")
        gain_hi_ready = sem("gain_hi_ready")
        gain_lo_ready = sem("gain_lo_ready")
        gain_spread = sem("gain_spread")
        gain_ready_act = sem("gain_ready_act")
        gain_ready_dve = sem("gain_ready_dve")
        params_loaded = sem("params_loaded")
        raw_loaded = [sem(f"raw_loaded{s}") for s in range(RING)]
        gate_w_loaded = sem("gate_w_loaded")
        y_loaded = sem("y_loaded")
        gout_loaded = sem("gout_loaded")
        stored = sem("stored")
        consts_ready = sem("consts_ready")
        fills_done = sem("fills_done")
        x_squared = sem("x_squared")
        x_var = sem("x_var")
        x_std = sem("x_std")
        xn_ready = sem("xn_ready")
        x_turned = sem("x_turned")
        h_hi_ready = sem("h_hi_ready")
        h_lo_ready = sem("h_lo_ready")
        params_turned = sem("params_turned")
        hi_ready = sem("hi_ready")
        lo_ready = sem("lo_ready")
        unit_used = sem("unit_used")
        v_done = sem("v_done")
        v_copied_act = sem("v_copied_act")
        v_copied_dve = sem("v_copied_dve")
        sp_neg = sem("sp_neg")
        sp_exp = sem("sp_exp")
        sp_ready = sem("sp_ready")
        sp_turned = sem("sp_turned")
        kq_hi_ready = sem("kq_hi_ready")
        kq_ready = sem("kq_ready")
        neg_c_ready = sem("neg_c_ready")
        neg_c_stored = sem("neg_c_stored")
        neg_c_loaded = [sem("neg_c_loaded0"), sem("neg_c_loaded1")]
        scores_done = sem("scores_done")
        c_summed = sem("c_summed")
        cq_copied = sem("cq_copied")
        score_read = sem("score_read")
        biased = sem("biased")
        masked = sem("masked")
        row_maxed = sem("row_maxed")
        max_ready = sem("max_ready")
        exp_done = sem("exp_done")
        inv_ready = sem("inv_ready")
        probs_ready = sem("probs_ready")
        probs_turned = sem("probs_turned")
        pT_hi_ready = sem("pT_hi_ready")
        pT_ready = sem("pT_ready")
        vh_hi_ready = sem("vh_hi_ready")
        vh_ready = sem("vh_ready")
        pv_done = sem("pv_done")
        pv_read = sem("pv_read")
        squared = sem("squared")
        sq_added = sem("sq_added")
        u_begun = sem("u_begun")
        taps = sem("taps")
        u_ready = sem("u_ready")
        u_hi_ready = sem("u_hi_ready")
        u_split = sem("u_split")
        gate_hi_ready = sem("gate_hi_ready")
        gate_ready = sem("gate_ready")
        gates_done = sem("gates_done")
        gates_read = sem("gates_read")
        iu_ready = sem("iu_ready")
        zl_sig = sem("zl_sig")
        zl_read = sem("zl_read")
        act_lru = sem("act_lru")
        decay_ready = sem("decay_ready")
        mult_sq = sem("mult_sq")
        mult_ready = sem("mult_ready")
        drive_ready = sem("drive_ready")
        h_ready = sem("h_ready")
        lru_done = sem("lru_done")
        za_sig = sem("za_sig")
        za_read = sem("za_read")
        mixA_done = sem("mixA_done")
        mix_hi_ready = sem("mix_hi_ready")
        mix_ready = sem("mix_ready")
        ssq_done = sem("ssq_done")
        g_var = sem("g_var")
        g_std = sem("g_std")
        g_rstd = sem("g_rstd")
        y_done = sem("y_done")
        y_read = sem("y_read")
        y_squared = sem("y_squared")
        y_gained = sem("y_gained")
        y_var = sem("y_var")
        y_std = sem("y_std")
        y_rstd = sem("y_rstd")
        y_final = sem("y_final")
        y_final_act = sem("y_final_act")
        dve_step = sem("dve_step")
        waits_passed = [sem("pool_waits_passed"), sem("sp_waits_passed")]

        def wait_alone(engine, semaphore, value):
            engine.wait_ge(semaphore, value).then_inc(waits_passed[engine is nc.sync], 1)

        KIND_A, KIND_B, KIND_C = (2, A_COLS), (KC // B_UNITS, B_COLS), (2, C_COLS)

        def slot(t, s, kind):
            return t[:, s, 0:kind[0] * kind[1]].rearrange("p (k n) -> p k n", k=kind[0])

        block = ctx.enter_context(nc.Block())

        @block.sync
        def _(sp):
            sp.dma_start(x_in[:, 0, 0:D // 2], x_tiles[0][:, 0:D // 2]).then_inc(x_half_loaded, 16)
            sp.dma_start(x_in[:, 0, D // 2:D], x_tiles[0][:, D // 2:D]).then_inc(x_loaded[0], 16)

            def fetch(s, kind, weights, row, col):
                rows = kind[0] * P
                sp.dma_start(slot(raw, s, kind), weights[row:row + rows, ds(col, kind[1])].rearrange(
                    "(k p) n -> p k n", p=P)).then_inc(raw_loaded[s], 16)

            for t in range(1, TT):
                for u in range(2 * t - 2, min(2 * t, RING)):
                    fetch(u, KIND_A, w_in2, 2 * P * u, A_FIRST)
                sp.dma_start(x_in[:, t, :], x_tiles[t]).then_inc(x_loaded[t], 16)
            for row, src in enumerate((conv_b, b_rg, b_ig, lru_lambda, attn_norm_g, lru_norm_g)):
                sp.dma_start(param_row[row * NH:(row + 1) * NH, :], src[0].rearrange("(n p) -> n p", p=P)
                             ).then_inc(params_loaded, 16)
            sp.dma_start(param_row[V_CONVW * NH:N_VEC * NH, :],
                         conv_w[0].rearrange("k (n p) -> (k n) p", p=P)).then_inc(params_loaded, 16)
            sp.dma_start(bf_all[:], b_f[0].partition_broadcast(P)).then_inc(params_loaded, 16)

            def load(n, s, kind, weights, row, col):
                wait_alone(sp, lo_ready, n + 1)
                fetch(s, kind, weights, row, col)

            for u in range(RING, A_UNITS):
                load(u, u % RING, KIND_A, w_in2, 2 * P * u, A_FIRST)
            with sp.Fori(1, A_GROUPS) as g:
                for u in range(A_UNITS):
                    load(g * A_UNITS + u, u % RING, KIND_A, w_in2, 2 * P * u,
                         A_FIRST - g * A_COLS)
            with sp.Fori(0, ROUNDS) as g:
                for s, col in enumerate((COL_K, COL_Q, COL_X, COL_ZL, COL_ZA)):
                    for u in range(B_UNITS):
                        load(g * SLOTS + (B0 + s * B_UNITS + u), u % RING, KIND_B,
                             w_in2, 4 * P * u, g * B_COLS + col)
                    if s == 1:
                        wait_alone(sp, gates_done, g * 2 + 1)
                        sp.dma_start(gate_w[:, 0:2, :], w_rg[0][ds(g * 2, 2)].rearrange("b c d -> c b d")
                                     ).then_inc(gate_w_loaded, 16)
                        sp.dma_start(gate_w[:, 2:4, :], w_ig[0][ds(g * 2, 2)].rearrange("b c d -> c b d")
                                     ).then_inc(gate_w_loaded, 16)
            with sp.Fori(0, QUARTERS) as q:
                for u in range(C_UNITS):
                    load(q * C_UNITS + (C0 + u), u % RING, KIND_C,
                         w_out2, 2 * P * u, q * C_COLS)
            for t in range(TT):
                for cols, scaled, count in ((FIRST, y_final, 2 * t + 1), (MIDDLE, y_final_act, t + 1),
                                            (LAST, y_final, 2 * t + 2)):
                    sp.wait_ge(scaled, count)
                    sp.dma_start(out_tiles[t][:, cols], y[:, t, cols]).then_inc(stored, 16)
            sp.wait_ge(stored, 3 * 16 * TT)

        @block.tensor
        def _(pe):
            def three(dst, a_hi, a_lo, b_hi, b_lo, start, stop):
                nc.tensor.matmul(dst, a_hi, b_hi, start=start, stop=False)
                nc.tensor.matmul(dst, a_hi, b_lo, start=False, stop=False)
                return nc.tensor.matmul(dst, a_lo, b_hi, start=False, stop=stop)

            pe.sem_inc(gates_done, 1)

            def turn_x(t):
                for b in range(4):
                    pe.wait_ge(xn_ready, 2 * t + b // 2 + 1)
                    if t >= 1:
                        pe.wait_ge(h_lo_ready, 4 * (t - 1) + b + 1)
                    for j in range(4):
                        k = 4 * b + j
                        mm = nc.tensor.transpose(bank[:, 4 + b, j * P:(j + 1) * P],
                                                 x_in[:, t, k * P:(k + 1) * P], ident[:])
                    mm.then_inc(x_turned, 1)

            def wide(dst, k, t, s, kk, kind, start, stop):
                if kind is KIND_C and k < 2:
                    hi, lo = first_hi[:, k], first_lo[:, k]
                else:
                    hi, lo = hT_hi[:, k], hT_lo[:, k]
                tok = slice(t * P, (t + 1) * P)
                return three(dst, hi[:, tok], lo[:, tok], slot(w_hi, s, kind)[:, kk, :],
                             slot(w_lo, s, kind)[:, kk, :], start, stop)

            pe.wait_ge(consts_ready, 1)
            for b in range(4):
                cols = slice(b * S, (b + 1) * S)
                pe.wait_ge(gain_hi_ready, b + 1)
                nc.tensor.matmul(bank[:, b, :], ones_row[:, :], gain_hi[:, cols], start=True, stop=False)
                pe.wait_ge(gain_lo_ready, b + 1)
                nc.tensor.matmul(bank[:, b, :], ones_row[:, :], gain_lo[:, cols], start=False, stop=True
                                 ).then_inc(gain_spread, 1)
            turn_x(0)
            turn_x(1)
            for half in range(2):
                for t in range(TT):
                    if half == 0:
                        pe.wait_ge(gain_ready_act, 2)
                        pe.wait_ge(gain_ready_dve, 2)
                    for u in range(4 * half, 4 * half + 4):
                        pe.wait_ge(lo_ready, u + 1 + CREDIT)
                        pe.wait_ge(h_lo_ready, 4 * t + u // 2 + 1)
                        for kk in range(2):
                            k = 2 * u + kk
                            mm = wide(bank[:, t, 0:A_COLS], k, t, u % RING, kk, KIND_A, k == 0, k == KC - 1)
                            if k == KC - 1 and t < TT - 1:
                                mm.then_inc(v_done, 1)
                        if t == TT - 1:
                            mm.then_inc(unit_used, 1)
                    if half == 0 and t < TT - 2:
                        turn_x(t + 2)
                    if half == 0 and t == TT - 1:
                        pe.wait_ge(params_loaded, 16 * 8)
                        nc.tensor.transpose(bank[:, 4, 0:N_VEC * NH], param_row[:, :],
                                            ident[0:N_VEC * NH, 0:N_VEC * NH]).then_inc(params_turned, 1)

            with pe.Fori(1, A_GROUPS) as g:
                for u in range(A_UNITS):
                    pe.wait_ge(lo_ready, g * A_UNITS + (u + 1 + CREDIT))
                    for kk in range(2):
                        k = 2 * u + kk
                        for t in range(TT):
                            if k == 0:
                                pe.wait_ge((v_copied_act, v_copied_dve)[t % 2], g * 2 + (t // 2 - 1))
                            mm = wide(bank[:, t, 0:A_COLS], k, t, u % RING, kk, KIND_A, k == 0, k == KC - 1)
                            if k == KC - 1 and t < TT - 1:
                                mm.then_inc(v_done, 1)
                    mm.then_inc(unit_used, 1)
            pe.wait_ge(sp_ready, 1)
            for t in range(TT):
                mm = nc.tensor.transpose(bank[0:NH, 7, t * P:(t + 1) * P], softp[:, t * NH:(t + 1) * NH],
                                         ident[:])
            mm.then_inc(sp_turned, 1)
            pe.wait_ge(consts_ready, 4)
            nc.tensor.matmul(bank[:, 6, 0:TT * NH], upper[:, :], softp[:, 0:TT * NH], start=True, stop=False)
            for back in range(1, TT):
                mm = nc.tensor.matmul(bank[:, 6, back * NH:TT * NH], ones[:, :],
                                      softp[:, 0:(TT - back) * NH], start=False, stop=back == TT - 1)
            mm.then_inc(c_summed, 1)
            pe.wait_ge(v_copied_act, 2 * A_GROUPS)
            pe.wait_ge(v_copied_dve, 2 * A_GROUPS)

            def unit(g, u, b0):
                pe.wait_ge(lo_ready, g * SLOTS + (B0 + u + 1 + CREDIT))
                hi, lo = slot(w_hi, u % RING, KIND_B), slot(w_lo, u % RING, KIND_B)
                for kk in range(4):
                    k = (u % B_UNITS) * 4 + kk
                    for c in range(2):
                        ch = slice(c * P, (c + 1) * P)
                        mm = three(bank[:, b0 + c, :], hi[:, kk, ch], lo[:, kk, ch], hT_hi[:, k, :],
                                   hT_lo[:, k, :], k == 0, k == KC - 1)
                mm.then_inc(unit_used, 1)

            def scores(g, c):
                if c == 0:
                    pe.wait_ge(za_read, g * 2 + 1)
                    pe.wait_ge(neg_c_ready, 1)
                    pe.wait_ge(cq_copied, 1)
                pe.wait_ge(kq_ready, g * 4 + (3 + c))
                for i in range(TT):
                    if c == 1:
                        pe.wait_ge(score_read, g * 8 + (i + 1))
                    rows, keys = slice(i * P, (i + 1) * P), slice(0, (i + 1) * P)
                    mm = three(bank[:, 4 + i, keys], q_hi[:, c, rows], q_lo[:, c, rows], k_hi[:, c, keys],
                               k_lo[:, c, keys], True, True)
                    mm.then_inc(scores_done, 1)

            def turn_probs(g, c):
                pe.wait_ge(probs_ready, g * 2 + (c + 1))
                if c == 0:
                    pe.wait_ge(score_read, g * 8 + 8)
                else:
                    pe.wait_ge(pT_ready, g * 6 + 3)
                for b, tiles in ((4, (0,)), (5, (1, 3)), (6, (2,))):
                    for j in tiles:
                        for i in range(j, TT):
                            at = PT_AT[j] - 512 * (b - 4) + (i - j) * P
                            mm = nc.tensor.transpose(bank[:, b, at:at + P],
                                                     probs[:, c, TRI[i] + j * P:TRI[i] + (j + 1) * P],
                                                     ident[:])
                    mm.then_inc(probs_turned, 1)

            def values(g, c):
                pe.wait_ge(pT_ready, g * 6 + 3 * (c + 1))
                pe.wait_ge(vh_ready, g * 2 + (c + 1))
                if c == 1:
                    pe.wait_ge(pv_read, g * 2 + 1)
                for j in range(TT):
                    cols = slice(PT_AT[j], PT_AT[j] + S - j * P)
                    mm = three(bank[:, 7, j * P:S], vh_hi[:, j, :], vh_lo[:, j, :], pT_hi[:, cols],
                               pT_lo[:, cols], j == 0, j == TT - 1)
                mm.then_inc(pv_done, 1)

            def gates(g, c):
                if c == 0:
                    pe.wait_ge(gate_ready, g + 1)
                    pe.wait_ge(u_split, g * 2 + 2)
                else:
                    pe.wait_ge(gates_read, g * 2 + 1)
                for gate in range(2):
                    mm = three(bank[:, gate, :], gate_hi[:, 2 * gate + c, :], gate_lo[:, 2 * gate + c, :],
                               u_hi[:, c, :], u_lo[:, c, :], True, True)
                mm.then_inc(gates_done, 1)

            with pe.Fori(0, ROUNDS) as g:
                for u in range(SLOTS):
                    if u in (9, 10):
                        scores(g, u - 9)
                    if u in (11, 13):
                        turn_probs(g, (u - 11) // 2)
                    if u in (12, 14):
                        values(g, (u - 12) // 2)
                    if u in (14, 15):
                        gates(g, u - 14)
                    if u == 18:
                        pe.wait_ge(gates_read, g * 2 + 2)
                    if u == 19:
                        pe.wait_ge(zl_read, g * 2 + 2)
                        pe.wait_ge(pv_read, g * 2 + 2)
                    unit(g, u, (0, 2, 0, 2, 4)[u // B_UNITS])

            pe.wait_ge(sq_added, 4 * ROUNDS)
            for i in range(2 * TT):
                mm = nc.tensor.matmul(bank[:, 6, i:i + 1], sum_sq[:, i // TT, (i % TT) * P:(i % TT + 1) * P],
                                      ones_col[:, :], start=True, stop=True)
            mm.then_inc(ssq_done, 1)

            def project(q, units, tiles):
                for u in units:
                    pe.wait_ge(lo_ready, q * C_UNITS + (C0 + u + 1 + CREDIT))
                    pe.wait_ge(mix_ready, 2 * u + 2)
                    half = u // (C_UNITS // 2)
                    for kk in range(2):
                        k = 2 * u + kk
                        first, last = k % NH == 0, k % NH == NH - 1
                        for t in tiles:
                            if first:
                                if half == 1 and t == 0:
                                    pe.wait_ge(za_read, 2 * ROUNDS + 1)
                                    pe.wait_ge(g_var, 1)
                                pe.wait_ge(y_read, q * 8 + (4 * half + t + 1))
                            mm = wide(bank[:, 4 * half + t, :], k, t, u % RING, kk, KIND_C, first, last)
                            if last and t < TT - 1:
                                mm.then_inc(y_done, 1)
                    if TT - 1 in tiles:
                        mm.then_inc(unit_used, 1)

            with pe.Fori(0, QUARTERS - 1) as q:
                project(q, range(C_UNITS), range(TT))
            project(QUARTERS - 1, range(C_UNITS // 2), range(TT))
            for t in range(TT):
                project(QUARTERS - 1, range(C_UNITS // 2, C_UNITS), (t,))

        @block.scalar
        def _(act):
            def activate(dst, src, f, **kw):
                return nc.scalar.activation(dst, src, f, **kw)

            def split_hi(n, s, cols, loads):
                act.wait_ge(raw_loaded[s], loads * 16)
                act.wait_ge(unit_used, n + 1)
                activate(w_hi[:, s, 0:cols], raw[:, s, 0:cols], ACT.Copy).then_inc(hi_ready, 1)

            act.sem_inc(unit_used, RING)

            act.dma_start(gain_row[:], norm_g).then_inc(gain_loaded, 16)
            act.wait_ge(fills_done, 2)
            activate(rstd_x[:, 0:1], ones[:, 0:1], ACT.Sqrt).then_inc(table_loaded, 1)
            activate(ones_row[:], ones[0:1, :], ACT.Copy)
            act.wait_ge(table_loaded, 1)
            act.wait_ge(gain_loaded, 16)
            for b in range(4):
                cols = slice(b * S, (b + 1) * S)
                activate(gain_hi[:, cols], gain_row[:, cols], ACT.Copy).then_inc(gain_hi_ready, 1)

            def square_x(t):
                if t == 0:
                    act.wait_ge(x_half_loaded, 16)
                    activate(junk[:, 0:D // 2], x_in[:, 0, 0:D // 2], ACT.Square, accum_out=ms_x0[:]
                             ).then_inc(x_half_squared, 1)
                    act.wait_ge(x_loaded[t], 16)
                    activate(junk[:, D // 2:D], x_in[:, 0, D // 2:D], ACT.Square, accum_out=ms_x[:, 0:1]
                             ).then_inc(x_squared, 1)
                    return
                act.wait_ge(x_loaded[t], 16)
                act.wait_ge(x_half_squared, 1)
                act.wait_ge(x_squared, t)
                activate(junk[:], x_in[:, t, :], ACT.Square, accum_out=ms_x[:, t:t + 1]
                         ).then_inc(x_squared, 1)

            def std_x(t):
                act.wait_ge(x_var, t + 1)
                activate(rstd_x[:, t:t + 1], rstd_x[:, t:t + 1], ACT.Sqrt).then_inc(x_std, 1)

            def h_hi(t):
                for b in range(4):
                    act.wait_ge(x_turned, 4 * t + b + 1)
                    activate(hT_hi[:, 4 * b:4 * b + 4, t * P:(t + 1) * P],
                             bank[:, 4 + b, :].rearrange("p (k n) -> p k n", k=4), ACT.Copy).then_inc(h_hi_ready, 1)

            for t in range(TT):
                square_x(t)
                std_x(t)
                if t < 2:
                    split_hi(2 * t, 2 * t, 2 * A_COLS, 1)
                if t == 0:
                    for b in (2, 3):
                        act.wait_ge(gain_spread, b + 1)
                        activate(gain_in[:, b * S:(b + 1) * S], bank[:, b, :], ACT.Copy).then_inc(gain_ready_act, 1)
                if t >= 1:
                    h_hi(t - 1)
                if t < 2:
                    split_hi(2 * t + 1, 2 * t + 1, 2 * A_COLS, 1)
            h_hi(TT - 1)

            def split_ahead(n):
                split_hi(n, n % RING, 2 * A_COLS if n < N_A else UCOLS, n // RING + 1)

            def copy_v(g):
                col = (A_GROUPS - 1 - g) * A_COLS
                for t in (0, 2):
                    act.wait_ge(v_done, 3 * g + t + 1)
                    activate(v_raw[:, t, col:col + A_COLS], bank[:, t, 0:A_COLS], ACT.Copy
                             ).then_inc(v_copied_act, 1)

            for g in range(A_GROUPS):
                for u in range(A_UNITS):
                    n = g * A_UNITS + u + AHEAD
                    if g == 0 and u == A_UNITS - 1:
                        copy_v(g)
                    if n >= RING:
                        split_ahead(n)
                    if g == 1 and u == 0:
                        act.wait_ge(sp_neg, 1)
                        activate(sp_e[:], sp_e[:], ACT.Exp).then_inc(sp_exp, 1)
                if g > 0:
                    copy_v(g)

            def split_round(g, u):
                n = B0 + u + AHEAD
                split_hi(g * SLOTS + n, n % RING, UCOLS, g * SLABS + (n // RING + 1))

            def to_hi(g, dst, b0, slot_end):
                act.wait_ge(unit_used, g * SLOTS + (B0 + slot_end + RING))
                for c in range(2):
                    activate(dst[:, c, :], bank[:, b0 + c, :], ACT.Copy).then_inc(kq_hi_ready, 1)

            def bias_scores(g, c):
                for i in range(TT):
                    act.wait_ge(scores_done, g * 8 + (4 * c + i + 1))
                    activate(probs[:, c, TRI[i]:TRI[i] + (i + 1) * P], bank[:, 4 + i, 0:(i + 1) * P],
                             ACT.Identity, bias=cq[:, i, ds(g * 2 + c, 1)], scale=SCALE).then_inc(score_read, 1)

            def exp_scores(g, c):
                act.wait_ge(max_ready, g * 2 + (c + 1))
                for i in range(TT):
                    block_ = probs[:, c, TRI[i]:TRI[i] + (i + 1) * P]
                    activate(block_, block_, ACT.Exp, bias=row_max[:, c, i:i + 1],
                             accum_out=row_sum[:, c, i:i + 1]).then_inc(exp_done, 1)

            def pT_to_hi(g, c):
                for b, n in ((0, 512), (1, 512), (2, 256)):
                    act.wait_ge(probs_turned, g * 6 + (3 * c + b + 1))
                    activate(pT_hi[:, 512 * b:512 * b + n], bank[:, 4 + b, 0:n], ACT.Copy
                             ).then_inc(pT_hi_ready, 1)

            def head_v_hi(g, c):
                activate(vh_hi[:], v_raw[:, :, ds(g * 2 * P + c * P, P)], ACT.Copy
                         ).then_inc(vh_hi_ready, 1)

            def head_out(g, c):
                act.wait_ge(pv_done, g * 2 + (c + 1))
                activate(squares[:, c, :], bank[:, 7, :], ACT.Square).then_inc(squared, 1)
                activate(mix[:, ds(g * 2 + c, 1), :], bank[:, 7:8, :], ACT.Copy).then_inc(pv_read, 1)

            def column(vec, g, c):
                return param[:, ds(g * 2 + (vec * NH + c), 1)]

            act.wait_ge(c_summed, 1)
            activate(cq[:], bank[:, 6, 0:TT * NH].rearrange("p (t h) -> p t h", t=TT), ACT.Copy, scale=-1.0
                     ).then_inc(cq_copied, 1)
            act.wait_ge(cq_copied, 1)
            act.wait_ge(neg_c_ready, 1)
            act.dma_start(neg_c_dram, neg_c[:]).then_inc(neg_c_stored, 16)
            act.wait_ge(neg_c_stored, 16)

            with act.Fori(0, ROUNDS) as g:
                for u in range(SLOTS):
                    split_round(g, u)
                    if u == 1:
                        for c in range(2):
                            act.dma_start(neg_c_head[:, c, :], neg_c_dram[ds(g * 2 + c, 1), :].rearrange(
                                "o s -> (o s)").partition_broadcast(P)).then_inc(neg_c_loaded[c], 16)
                    if u == 4:
                        to_hi(g, k_hi, 0, 4)
                    if u == 8:
                        to_hi(g, q_hi, 2, 8)
                    if u == 9:
                        head_v_hi(g, 0)
                        bias_scores(g, 0)
                    if u == 10:
                        exp_scores(g, 0)
                        bias_scores(g, 1)
                    if u == 11:
                        pT_to_hi(g, 0)
                        exp_scores(g, 1)
                    if u == 12:
                        act.wait_ge(unit_used, g * SLOTS + (B0 + 12 + RING))
                        for c in range(2):
                            activate(u_conv[:, c, :], bank[:, c, :], ACT.Identity,
                                     bias=column(V_CONVB, g, c), scale=column(V_CONVW + 3, g, c)
                                     ).then_inc(u_begun, 1)
                        head_out(g, 0)
                        head_v_hi(g, 1)
                        act.wait_ge(gate_w_loaded, g * 32 + 32)
                        activate(gate_hi[:], gate_w[:], ACT.Copy).then_inc(gate_hi_ready, 1)
                    if u == 13:
                        pT_to_hi(g, 1)
                        for c in range(2):
                            act.wait_ge(u_ready, g * 2 + (c + 1))
                            activate(u_hi[:, c, :], u_conv[:, c, :], ACT.Copy).then_inc(u_hi_ready, 1)
                    if u == 14:
                        head_out(g, 1)
                    if u in (14, 15):
                        for c in (u - 14,):
                            act.wait_ge(gates_done, g * 2 + (c + 2))
                            activate(r_gate[:, c, :], bank[:, 0, :], ACT.Sigmoid, bias=column(V_BR, g, c)
                                     ).then_inc(act_lru, 1)
                            activate(i_gate[:, c, :], bank[:, 1, :], ACT.Sigmoid, bias=column(V_BI, g, c)
                                     ).then_inc(gates_read, 1)
                    if u == 16:
                        act.wait_ge(unit_used, g * SLOTS + (B0 + 16 + RING))
                        for c in range(2):
                            activate(z_sig[:, c, :], bank[:, 2 + c, :], ACT.Sigmoid).then_inc(zl_sig, 1)
                        act.wait_ge(act_lru, g * 2 + 2)
                        act.wait_ge(iu_ready, g * 2 + 2)
                        for c in range(2):
                            activate(decay[:, c, :], r_gate[:, c, :], ACT.Exp,
                                     scale=neg_s8[:, ds(g * 2 + c, 1)]).then_inc(decay_ready, 1)
                            activate(r_gate[:, c, :], r_gate[:, c, :], ACT.Tanh,
                                     scale=s8[:, ds(g * 2 + c, 1)])
                            act.wait_ge(decay_ready, g * 4 + (2 * c + 1))
                            activate(u_conv[:, c, :], decay[:, c, :], ACT.Square
                                     ).then_inc(decay_ready, 1)
                    if u == 17:
                        for c in range(2):
                            act.wait_ge(mult_sq, g * 2 + (c + 1))
                            activate(r_gate[:, c, :], r_gate[:, c, :], ACT.Sqrt).then_inc(mult_ready, 1)
                    if u == 18:
                        for c in range(2):
                            act.wait_ge(h_ready, g * 2 + (c + 1))
                            act.wait_ge(sq_added, g * 4 + (c + 1))
                            activate(squares[:, c:c + 1, :], mix[:, ds(g * 2 + (NH + c), 1), :],
                                     ACT.Square).then_inc(squared, 1)
                        with act.If_eq(act.to_reg(g), ROUNDS - 1):
                            for k in range(2):
                                activate(first_hi[:, k, :], mix[:, k, :], ACT.Copy).then_inc(mix_hi_ready, 1)
                    if u == 19:
                        act.wait_ge(lru_done, g * 2 + 2)
                        act.wait_ge(sq_added, g * 4 + 4)
                        act.wait_ge(unit_used, g * SLOTS + (B0 + 20 + RING))
                        for c in range(2):
                            activate(z_sig[:, c, :], bank[:, 4 + c, :], ACT.Sigmoid).then_inc(za_sig, 1)

            def mix_hi(k):
                if k == NH - 2:
                    act.wait_ge(mixA_done, 2 * ROUNDS)
                activate(hT_hi[:, k, :], mix[:, k, :], ACT.Copy).then_inc(mix_hi_ready, 1)

            act.wait_ge(unit_used, C0 + RING)
            for u in range(C_UNITS):
                if u == 0:
                    mix_hi(2)
                    mix_hi(3)
                split_ahead(C0 + u + AHEAD)
                if 1 <= u < 4:
                    for k in range(4 * u, 4 * u + 4):
                        mix_hi(k)
                if u == 1:
                    act.wait_ge(g_var, 1)
                    activate(rstd_g[:], rstd_g[:], ACT.Sqrt).then_inc(g_std, 1)
                if u == 4:
                    act.wait_ge(mix_ready, KC)
                    act.dma_start(y[:], x[0].rearrange("(t p) d -> p t d", p=P)).then_inc(y_loaded, 16)
                    act.dma_start(gain_out[:], final_norm_g.partition_broadcast(P)).then_inc(gout_loaded, 16)

            def square_y(q, after=None):
                for t in range(TT):
                    act.wait_ge(y_read, q * 8 + (8 + 4 + t + 1))
                    activate(junk[:, t * C_COLS:(t + 1) * C_COLS], y[:, t, ds(q * C_COLS, C_COLS)], ACT.Square,
                             accum_out=ms_y[:, t, ds(q, 1)]).then_inc(y_squared, 1)
                    if after:
                        after(t)
                act.wait_ge(y_squared, q * TT + TT)

            with act.Fori(1, QUARTERS - 1) as q:
                for u in range(C_UNITS):
                    n = C0 + u + AHEAD
                    split_hi(q * C_UNITS + n, n % RING, UCOLS, q * 2 + (n // RING + 1))
                    if u == 1:
                        square_y(q - 1)
            q = QUARTERS - 1
            for u in range(C_UNITS - AHEAD):
                split_ahead(C0 + q * C_UNITS + u + AHEAD)
                if u == 1:
                    square_y(q - 1)

            def scale_y(t):
                act.wait_ge(y_var, t + 1)
                activate(rstd_y[:, t:t + 1], rstd_y[:, t:t + 1], ACT.Sqrt).then_inc(y_std, 1)

                act.wait_ge(y_rstd, t + 1)
                activate(y[:, t, MIDDLE], y[:, t, MIDDLE], ACT.Copy, scale=rstd_y[:, t:t + 1]
                         ).then_inc(y_final_act, 1)

            act.wait_ge(y_gained, q * TT)
            square_y(q, scale_y)

        @block.gpsimd
        def _(pool):
            nc.gpsimd.memset(ident[:], 0.0).then_inc(fills_done, 1)
            nc.gpsimd.memset(ones[:], 1.0).then_inc(fills_done, 1)
            pool.wait_ge(fills_done, 2)
            nc.gpsimd.affine_select(out=ident[:], in_=ident[:], compare_op=ALU.not_equal, fill=1.0,
                                    base=0, pattern=[[-1, P]], channel_multiplier=1).then_inc(consts_ready, 1)
            nc.gpsimd.affine_select(out=upper[:], in_=ones[:], compare_op=ALU.is_ge, fill=0.0,
                                    base=0, pattern=[[1, P]], channel_multiplier=-1).then_inc(consts_ready, 1)
            nc.gpsimd.memset(ones_col[:], 1.0).then_inc(consts_ready, 1)
            nc.gpsimd.memset(sum_sq[:], 0.0).then_inc(consts_ready, 1)
            for n in range(RING):
                pool.wait_ge(hi_ready, n + 1)
                nc.gpsimd.tensor_tensor(w_lo[:, n, 0:2 * A_COLS], raw[:, n, 0:2 * A_COLS],
                                        w_hi[:, n, 0:2 * A_COLS].bitcast(F32), ALU.subtract
                                        ).then_inc(lo_ready, 1)

            def mask(g, c):
                for i in range(TT):
                    wait_alone(pool, biased, g * 8 + (4 * c + i + 1))
                    at = TRI[i] + i * P
                    nc.gpsimd.affine_select(out=probs[:, c, at:at + P], in_=probs[:, c, at:at + P],
                                            compare_op=ALU.is_ge, fill=masked_fill, base=0,
                                            pattern=[[-1, P]], channel_multiplier=1).then_inc(masked, 1)

            def add_squares(g, group, c):
                pool.wait_ge(squared, g * 4 + (2 * group + c + 1))
                if c:
                    pool.wait_ge(sq_added, g * 4 + (2 * group + c))
                nc.gpsimd.tensor_tensor(sum_sq[:, group, :], sum_sq[:, group, :], squares[:, c, :],
                                        ALU.add).then_inc(sq_added, 1)

            masked_fill = nc.gpsimd.to_reg(MASKED)
            with pool.Fori(0, ROUNDS) as g:
                mask(g, 0)
                mask(g, 1)
                for group in range(2):
                    for c in range(2):
                        add_squares(g, group, c)
                pool.wait_ge(sq_added, g * 4 + 4)

            with pool.Fori(0, QUARTERS - 1) as q:
                pool.wait_ge(gout_loaded, 16)
                for t in range(TT):
                    pool.wait_ge(y_squared, q * TT + (t + 1))
                    chunk = y[:, t, ds(q * C_COLS, C_COLS)]
                    nc.gpsimd.tensor_tensor(chunk, chunk, gain_out[:, ds(q * C_COLS, C_COLS)], ALU.mult
                                            ).then_inc(y_gained, 1)

        @block.vector
        def _(dve):
            steps = [0]

            def step(ins):
                steps[0] += 1
                ins.then_inc(dve_step, 1)
                dve.wait_ge(dve_step, steps[0])

            def split_lo(n, s, cols):
                dve.wait_ge(hi_ready, n + 1)
                nc.vector.tensor_tensor(w_lo[:, s, 0:cols], raw[:, s, 0:cols], w_hi[:, s, 0:cols].bitcast(F32),
                                        ALU.subtract).then_inc(lo_ready, 1)

            def split_ahead(n):
                split_lo(n, n % RING, 2 * A_COLS if n < N_A else UCOLS)

            dve.sem_inc(lo_ready, CREDIT)
            dve.sem_inc(za_read, 1)
            dve.sem_inc(y_read, 8)

            def normalise(t):
                dve.wait_ge(x_squared, t + 1)
                if t == 0:
                    dve.wait_ge(x_half_squared, 1)
                    step(nc.vector.tensor_tensor(ms_x[:, 0:1], ms_x[:, 0:1], ms_x0[:], ALU.add))
                nc.vector.tensor_scalar(rstd_x[:, t:t + 1], ms_x[:, t:t + 1], 1.0 / D, EPS, ALU.mult,
                                        ALU.add).then_inc(x_var, 1)
                dve.wait_ge(x_std, t + 1)
                step(nc.vector.reciprocal(rstd_x[:, t:t + 1], rstd_x[:, t:t + 1]))
                for cols, gain_ready in ((slice(0, D // 2), gain_ready_dve), (slice(D // 2, D), gain_ready_act)):
                    dve.wait_ge(gain_ready, 2)
                    nc.vector.scalar_tensor_tensor(out=x_in[:, t, cols], in0=x_in[:, t, cols],
                                                   scalar=rstd_x[:, t:t + 1], in1=gain_in[:, cols],
                                                   op0=ALU.mult, op1=ALU.mult).then_inc(xn_ready, 1)

            def h_lo(t):
                for b in range(4):
                    dve.wait_ge(h_hi_ready, 4 * t + b + 1)
                    out_ = (slice(None), slice(4 * b, 4 * b + 4), slice(t * P, (t + 1) * P))
                    nc.vector.tensor_tensor(hT_lo[out_], bank[:, 4 + b, :].rearrange(
                        "p (k n) -> p k n", k=4), hT_hi[out_].bitcast(F32), ALU.subtract).then_inc(h_lo_ready, 1)

            for b in range(4):
                cols = slice(b * S, (b + 1) * S)
                dve.wait_ge(gain_hi_ready, b + 1)
                nc.vector.tensor_tensor(gain_lo[:, cols], gain_row[:, cols], gain_hi[:, cols].bitcast(F32),
                                        ALU.subtract).then_inc(gain_lo_ready, 1)
            for b in range(2):
                dve.wait_ge(gain_spread, b + 1)
                nc.vector.tensor_copy(gain_in[:, b * S:(b + 1) * S], bank[:, b, :]).then_inc(gain_ready_dve, 1)

            for t in range(TT):
                normalise(t)
                if t >= 1:
                    h_lo(t - 1)
            h_lo(TT - 1)

            def softplus_begin():
                dve.wait_ge(v_copied_act, 2)
                dve.wait_ge(v_copied_dve, 2)
                dve.wait_ge(params_turned, 1)
                step(nc.vector.tensor_copy(param[:], bank[:, 4, 0:N_VEC * NH]))
                for t in range(TT):
                    nc.vector.tensor_tensor(sp_in[:, t * NH:(t + 1) * NH], v_raw[:, t, W:W + NH], bf_all[:],
                                            ALU.add)
                step(nc.vector.tensor_copy(sp_in[:, TT * NH:SPC], param[:, V_LAM * NH:(V_LAM + 1) * NH]))
                nc.vector.scalar_tensor_tensor(out=sp_e[:], in0=sp_in[:], scalar=-1.0, in1=sp_in[:],
                                               op0=ALU.mult, op1=ALU.min).then_inc(sp_neg, 1)

            def softplus_end():
                dve.wait_ge(sp_exp, 1)
                step(nc.vector.tensor_scalar(sp_s[:], sp_e[:], 2.0, None, ALU.add))
                step(nc.vector.reciprocal(sp_s[:], sp_s[:]))
                step(nc.vector.tensor_tensor(sp_s[:], sp_s[:], sp_e[:], ALU.mult))
                step(nc.vector.tensor_tensor(sp_s2[:], sp_s[:], sp_s[:], ALU.mult))
                step(nc.vector.tensor_scalar(sp_q[:], sp_s2[:], ATANH[0], None, ALU.mult))
                for a in ATANH[1:]:
                    step(nc.vector.scalar_tensor_tensor(out=sp_q[:], in0=sp_q[:], scalar=a, in1=sp_s2[:],
                                                        op0=ALU.add, op1=ALU.mult))
                step(nc.vector.scalar_tensor_tensor(out=sp_q[:], in0=sp_q[:], scalar=1.0, in1=sp_s[:],
                                                    op0=ALU.add, op1=ALU.mult))
                step(nc.vector.tensor_scalar(sp_in[:], sp_in[:], -1.0, 0.0, ALU.mult, ALU.max))
                step(nc.vector.scalar_tensor_tensor(out=softp[:], in0=sp_q[:], scalar=2.0, in1=sp_in[:],
                                                    op0=ALU.mult, op1=ALU.add))
                nc.vector.tensor_scalar(s8[:], softp[:, TT * NH:SPC], LRU_C, None, ALU.mult)
                step(nc.vector.tensor_scalar(neg_s8[:], softp[:, TT * NH:SPC], -LRU_C, None, ALU.mult))
                dve.sem_inc(sp_ready, 1)

            def copy_v(g, tiles):
                col = (A_GROUPS - 1 - g) * A_COLS
                for t in tiles:
                    if t == 3:
                        dve.wait_ge(unit_used, (g + 1) * A_UNITS + RING)
                    else:
                        dve.wait_ge(v_done, 3 * g + t + 1)
                    nc.vector.tensor_copy(v_raw[:, t, col:col + A_COLS], bank[:, t, 0:A_COLS]
                                          ).then_inc(v_copied_dve, 1)

            for g in range(A_GROUPS):
                for u in range(A_UNITS):
                    n = g * A_UNITS + u + AHEAD
                    if g == 0 and u == A_UNITS - 1:
                        copy_v(g, (1,))
                    if n >= RING:
                        split_ahead(n)
                    if g == 1 and u == 0:
                        softplus_begin()
                    if g == 1 and u == 1:
                        softplus_end()
                copy_v(g, (1, 3) if g else (3,))
            dve.wait_ge(sp_turned, 1)
            step(nc.vector.memset(neg_c_head[0:NH, 0, :], 1.0))
            nc.vector.tensor_tensor_scan(neg_c[:], neg_c_head[0:NH, 0, :], bank[0:NH, 7, :], 0.0,
                                         ALU.mult, ALU.add).then_inc(neg_c_ready, 1)

            def to_lo(g, b0, hi, lo, first):
                for c in range(2):
                    dve.wait_ge(kq_hi_ready, g * 4 + (first + c + 1))
                    nc.vector.tensor_tensor(lo[:, c, :], bank[:, b0 + c, :], hi[:, c, :].bitcast(F32),
                                            ALU.subtract).then_inc(kq_ready, 1)

            def head_v_lo(g, c):
                dve.wait_ge(vh_hi_ready, g * 2 + (c + 1))
                nc.vector.tensor_tensor(vh_lo[:], v_raw[:, :, ds(g * 2 * P + c * P, P)],
                                        vh_hi[:].bitcast(F32), ALU.subtract).then_inc(vh_ready, 1)

            def bias_keys(g, c):
                dve.wait_ge(neg_c_loaded[c], g * 16 + 16)
                for i in range(TT):
                    dve.wait_ge(score_read, g * 8 + (4 * c + i + 1))
                    row = probs[:, c, TRI[i]:TRI[i] + (i + 1) * P]
                    nc.vector.tensor_tensor(row, row, neg_c_head[:, c, 0:(i + 1) * P], ALU.add
                                            ).then_inc(biased, 1)
                for i in range(TT):
                    dve.wait_ge(masked, g * 8 + (4 * c + i + 1))
                    nc.vector.reduce_max(row_sum[:, c, i:i + 1], probs[:, c, TRI[i]:TRI[i] + (i + 1) * P],
                                         AX_X).then_inc(row_maxed, 1)
                dve.wait_ge(row_maxed, g * 8 + (4 * c + 4))
                nc.vector.tensor_scalar(row_max[:, c, :], row_sum[:, c, :], -1.0, None, ALU.mult
                                        ).then_inc(max_ready, 1)

            def normalise_probs(g, c):
                dve.wait_ge(exp_done, g * 8 + (4 * c + 4))
                nc.vector.reciprocal(row_inv[:, c, :], row_sum[:, c, :]).then_inc(inv_ready, 1)
                dve.wait_ge(inv_ready, g * 2 + (c + 1))
                for i in range(TT):
                    row = probs[:, c, TRI[i]:TRI[i] + (i + 1) * P]
                    ins = nc.vector.tensor_scalar(row, row, row_inv[:, c, i:i + 1], None, ALU.mult)
                ins.then_inc(probs_ready, 1)

            def pT_to_lo(g, c):
                for b, n in ((0, 512), (1, 512), (2, 256)):
                    dve.wait_ge(pT_hi_ready, g * 6 + (3 * c + b + 1))
                    cols = slice(512 * b, 512 * b + n)
                    nc.vector.tensor_tensor(pT_lo[:, cols], bank[:, 4 + b, 0:n], pT_hi[:, cols].bitcast(F32),
                                            ALU.subtract).then_inc(pT_ready, 1)

            def column(vec, g, c):
                return param[:, ds(g * 2 + (vec * NH + c), 1)]

            def convolve(g):
                for back in range(1, 4):
                    for c in range(2):
                        if back == 1:
                            dve.wait_ge(u_begun, g * 2 + (c + 1))
                        else:
                            dve.wait_ge(taps, g * 4 + (2 * (back - 2) + c + 1))
                        nc.vector.scalar_tensor_tensor(
                            out=u_conv[:, c, back:S], in0=bank[:, c, 0:S - back],
                            scalar=column(V_CONVW + 3 - back, g, c), in1=u_conv[:, c, back:S],
                            op0=ALU.mult, op1=ALU.add).then_inc(u_ready if back == 3 else taps, 1)

            with dve.Fori(0, ROUNDS) as g:
                for u in range(SLOTS):
                    n = B0 + u + AHEAD
                    split_lo(g * SLOTS + n, n % RING, UCOLS)
                    if u == 4:
                        to_lo(g, 0, k_hi, k_lo, 0)
                    if u == 8:
                        to_lo(g, 2, q_hi, q_lo, 2)
                    if u == 9:
                        head_v_lo(g, 0)
                        bias_keys(g, 0)
                    if u == 10:
                        normalise_probs(g, 0)
                        bias_keys(g, 1)
                    if u == 11:
                        pT_to_lo(g, 0)
                        normalise_probs(g, 1)
                    if u == 12:
                        convolve(g)
                        head_v_lo(g, 1)
                        dve.wait_ge(gate_hi_ready, g + 1)
                        nc.vector.tensor_tensor(gate_lo[:], gate_w[:], gate_hi[:].bitcast(F32),
                                                ALU.subtract).then_inc(gate_ready, 1)
                    if u == 13:
                        pT_to_lo(g, 1)
                        for c in range(2):
                            dve.wait_ge(u_hi_ready, g * 2 + (c + 1))
                            nc.vector.tensor_tensor(u_lo[:, c, :], u_conv[:, c, :], u_hi[:, c, :].bitcast(F32),
                                                    ALU.subtract).then_inc(u_split, 1)
                    if u == 15:
                        for c in range(2):
                            dve.wait_ge(gates_read, g * 2 + (c + 1))
                            nc.vector.tensor_tensor(i_gate[:, c, :], i_gate[:, c, :], u_conv[:, c, :],
                                                    ALU.mult).then_inc(iu_ready, 1)
                    if u == 16:
                        for c in range(2):
                            dve.wait_ge(zl_sig, g * 2 + (c + 1))
                            nc.vector.tensor_tensor(z_sig[:, c, :], bank[:, 2 + c, :], z_sig[:, c, :],
                                                    ALU.mult).then_inc(zl_read, 1)
                        for c in range(2):
                            dve.wait_ge(decay_ready, g * 4 + (2 * c + 2))
                            nc.vector.scalar_tensor_tensor(out=r_gate[:, c, :], in0=u_conv[:, c, :],
                                                           scalar=1.0, in1=r_gate[:, c, :], op0=ALU.add,
                                                           op1=ALU.mult).then_inc(mult_sq, 1)
                    if u == 17:
                        for c in range(2):
                            dve.wait_ge(mult_ready, g * 2 + (c + 1))
                            nc.vector.tensor_tensor(i_gate[:, c, :], i_gate[:, c, :], r_gate[:, c, :],
                                                    ALU.mult).then_inc(drive_ready, 1)
                        for c in range(2):
                            dve.wait_ge(drive_ready, g * 2 + (c + 1))
                            nc.vector.tensor_tensor_scan(mix[:, ds(g * 2 + (NH + c), 1), :].rearrange(
                                "p o s -> p (o s)"), decay[:, c, :], i_gate[:, c, :], 0.0, ALU.mult,
                                ALU.add).then_inc(h_ready, 1)
                    if u == 18:
                        for c in range(2):
                            dve.wait_ge(squared, g * 4 + (3 + c))
                            tile = mix[:, ds(g * 2 + (NH + c), 1), :]
                            nc.vector.scalar_tensor_tensor(out=tile, in0=tile, scalar=column(V_GL, g, c),
                                                           in1=z_sig[:, c:c + 1, :], op0=ALU.mult,
                                                           op1=ALU.mult).then_inc(lru_done, 1)
                        with dve.If_eq(dve.to_reg(g), ROUNDS - 1):
                            for k in range(2):
                                dve.wait_ge(mix_hi_ready, k + 1)
                                nc.vector.tensor_tensor(first_lo[:, k, :], mix[:, k, :],
                                                        first_hi[:, k, :].bitcast(F32), ALU.subtract
                                                        ).then_inc(mix_ready, 1)
                    if u == 19:
                        for c in range(2):
                            dve.wait_ge(za_sig, g * 2 + (c + 1))
                            nc.vector.tensor_tensor(z_sig[:, c, :], bank[:, 4 + c, :], z_sig[:, c, :],
                                                    ALU.mult).then_inc(za_read, 1)
                        for c in range(2):
                            dve.wait_ge(za_read, g * 2 + (c + 2))
                            tile = mix[:, ds(g * 2 + c, 1), :]
                            nc.vector.scalar_tensor_tensor(out=tile, in0=tile, scalar=column(V_GA, g, c),
                                                           in1=z_sig[:, c:c + 1, :], op0=ALU.mult,
                                                           op1=ALU.mult).then_inc(mixA_done, 1)

            def mix_lo(k):
                dve.wait_ge(mix_hi_ready, k + 1)
                nc.vector.tensor_tensor(hT_lo[:, k, :], mix[:, k, :], hT_hi[:, k, :].bitcast(F32),
                                        ALU.subtract).then_inc(mix_ready, 1)

            def add_half(q, half, tiles=range(TT)):
                for t in tiles:
                    if t == TT - 1:
                        dve.wait_ge(unit_used, q * C_UNITS + (C0 + (half + 1) * C_UNITS // 2 + RING))
                    else:
                        dve.wait_ge(y_done, q * 6 + (3 * half + t + 1))
                    chunk = y[:, t, ds(q * C_COLS, C_COLS)]
                    if half == 1:
                        dve.wait_ge(y_read, q * 8 + (8 + t + 1))
                    nc.vector.scalar_tensor_tensor(out=chunk, in0=bank[:, 4 * half + t, :],
                                                   scalar=rstd_g[:, 4 * half + t:4 * half + t + 1],
                                                   in1=chunk, op0=ALU.mult, op1=ALU.add).then_inc(y_read, 1)

            for u in range(C_UNITS):
                if u == 0:
                    mix_lo(2)
                    mix_lo(3)
                split_ahead(C0 + u + AHEAD)
                if u == 0:
                    dve.wait_ge(ssq_done, 1)
                    nc.vector.tensor_scalar(rstd_g[:], bank[:, 6, 0:2 * TT], 1.0 / W, EPS, ALU.mult,
                                            ALU.add).then_inc(g_var, 1)
                if 1 <= u < 4:
                    for k in range(4 * u, 4 * u + 4):
                        mix_lo(k)
                if u == 2:
                    dve.wait_ge(g_std, 1)
                    nc.vector.reciprocal(rstd_g[:], rstd_g[:]).then_inc(g_rstd, 1)
                if u == 5:
                    dve.wait_ge(g_rstd, 1)
                    dve.wait_ge(y_loaded, 16)
                    add_half(0, 0)
            add_half(0, 1)
            with dve.Fori(1, QUARTERS - 1) as q:
                for u in range(C_UNITS):
                    n = C0 + u + AHEAD
                    split_lo(q * C_UNITS + n, n % RING, UCOLS)
                    if u == 4:
                        add_half(q, 0)
                add_half(q, 1)
            q = QUARTERS - 1
            for u in range(C_UNITS - AHEAD):
                split_ahead(C0 + q * C_UNITS + u + AHEAD)
                if u == 4:
                    add_half(q, 0)
            dve.wait_ge(gout_loaded, 16)
            dve.wait_ge(y_gained, (QUARTERS - 1) * TT)
            dve.wait_ge(y_squared, q * TT)
            step(nc.vector.reduce_sum(ms_first[:], ms_y[:, :, 0:q], AX_X))
            step(nc.vector.tensor_scalar(ms_first[:], ms_first[:], 1.0 / D, EPS, ALU.mult, ALU.add))
            for t in range(TT):
                add_half(q, 1, (t,))
                dve.wait_ge(y_squared, q * TT + t + 1)
                nc.vector.scalar_tensor_tensor(out=rstd_y[:, t:t + 1], in0=ms_y[:, t, q:q + 1],
                                               scalar=1.0 / D, in1=ms_first[:, t:t + 1], op0=ALU.mult,
                                               op1=ALU.add).then_inc(y_var, 1)
                dve.wait_ge(y_std, t + 1)
                nc.vector.reciprocal(rstd_y[:, t:t + 1], rstd_y[:, t:t + 1]).then_inc(y_rstd, 1)
                dve.wait_ge(y_rstd, t + 1)
                nc.vector.tensor_scalar(y[:, t, FIRST], y[:, t, FIRST], rstd_y[:, t:t + 1], None, ALU.mult
                                        ).then_inc(y_final, 1)
                nc.vector.scalar_tensor_tensor(out=y[:, t, LAST], in0=y[:, t, LAST],
                                               scalar=rstd_y[:, t:t + 1], in1=gain_out[:, LAST],
                                               op0=ALU.mult, op1=ALU.mult).then_inc(y_final, 1)


_INS = ['x', 'norm_g', 'w_in', 'b_f', 'conv_w', 'conv_b', 'w_rg', 'b_rg', 'w_ig', 'b_ig', 'lru_lambda',
        'attn_norm_g', 'lru_norm_g', 'w_out', 'final_norm_g']


def kernel(**inputs):
    import numpy as np
    import concourse.bacc as bacc
    from concourse.bass_utils import run_bass_kernel_spmd

    nc = bacc.Bacc("TRN2", target_bir_lowering=False, num_devices=1, dynamic_dma_scratch_size=1024)
    arrays, args = {}, []
    for name in _INS:
        a = np.ascontiguousarray(inputs[name])
        arrays[f"in_{name}_dram"] = a
        args.append(nc.dram_tensor(f"in_{name}_dram", a.shape, mybir.dt.from_np(a.dtype),
                                   kind="ExternalInput").ap())
    args.append(nc.dram_tensor("out_dram", inputs['x'].shape, F32, kind="ExternalOutput").ap())
    hybrid_layer(nc, *args)
    r = run_bass_kernel_spmd(nc, [arrays], core_ids=[0])
    return r.results[0]["out_dram"]
```
